# Optimizing a Trainium2 kernel written in Bass

```python
import math
import jax, jax.numpy as jnp
from jax import lax
import numpy as np

D_MODEL = 1024
BATCH = 1
SEQ = 256
DEPTH = 2

CHUNK = 64
Q_BLOCK = 128
HEAD_DIM = 64
A_Q_HEADS = D_MODEL // (2 * HEAD_DIM)
A_KV_HEADS = A_Q_HEADS // 4
WINDOW = 128
WINDOW_CHUNKS = WINDOW // CHUNK
B_HEADS = D_MODEL // (2 * HEAD_DIM)
C_HEADS = D_MODEL // HEAD_DIM
MEM_LEN = 256
MEM_HEADS = 4
MEM_HEAD_DIM = D_MODEL // MEM_HEADS
D_FF = 256 * ((8 * D_MODEL // 3 + 255) // 256)
N_EXPERTS = 8
TOP_K = 2
D_EXPERT = 7 * D_MODEL // 2
N_EVEN = (DEPTH + 1) // 2
N_ODD = DEPTH // 2
ALPHA = (2.0 * DEPTH) ** 0.25
BETA = (8.0 * DEPTH) ** -0.25
LN_EPS = 1e-5
FORGET_BIAS_INIT = 3.0
AB_SPLITS = (A_Q_HEADS * HEAD_DIM, A_KV_HEADS * HEAD_DIM, A_KV_HEADS * HEAD_DIM,
             B_HEADS * HEAD_DIM, B_HEADS * HEAD_DIM, B_HEADS * HEAD_DIM)
AB_IN = sum(AB_SPLITS)
AB_OUT = (A_Q_HEADS + B_HEADS) * HEAD_DIM
C_SPLITS = (C_HEADS * HEAD_DIM, C_HEADS * HEAD_DIM, C_HEADS * HEAD_DIM, C_HEADS)
C_IN = sum(C_SPLITS)
C_OUT = C_HEADS * HEAD_DIM

kernel_name = "hybrid_chunk_causal_swa_stickbreak_fox_moe_deepnorm"

def split_cols(proj, sizes):
    offsets = np.cumsum(sizes)[:-1].tolist()
    return jnp.split(proj, offsets, axis=-1)

def layer_norm(x, g, b):
    xf = x.astype(jnp.float32)
    mu = jnp.mean(xf, axis=-1, keepdims=True)
    var = jnp.mean(jnp.square(xf - mu), axis=-1, keepdims=True)
    return ((xf - mu) * lax.rsqrt(var + LN_EPS)).astype(x.dtype) * g + b

def alibi_slopes(n_heads):
    return 2.0 ** (-8.0 * jnp.arange(1, n_heads + 1, dtype=jnp.float32) / n_heads)

def sliding_window_gqa_sinks(q, k, v, sinks):
    bsz, seq, n_h, dh = q.shape
    n_kv = k.shape[2]
    grp = n_h // n_kv
    nc = seq // CHUNK
    w = WINDOW_CHUNKS
    band = w * CHUNK
    qc = q.reshape(bsz, nc, CHUNK, n_kv, grp, dh)
    pad = ((0, 0), ((w - 1) * CHUNK, 0), (0, 0), (0, 0))
    kc = jnp.pad(k, pad).reshape(bsz, nc + w - 1, CHUNK, n_kv, dh)
    vc = jnp.pad(v, pad).reshape(bsz, nc + w - 1, CHUNK, n_kv, dh)
    kb = jnp.concatenate([kc[:, i:i + nc] for i in range(w)], axis=2)
    vb = jnp.concatenate([vc[:, i:i + nc] for i in range(w)], axis=2)
    scores = jnp.einsum('bcqkgd,bcskd->bckgqs', qc, kb).astype(jnp.float32) * (dh ** -0.5)
    qi = jnp.arange(CHUNK)
    kj = jnp.arange(band)
    dist = jnp.abs(qi[:, None] + (w - 1) * CHUNK - kj[None, :]).astype(jnp.float32)
    bias = (-alibi_slopes(n_h)[:, None, None] * dist[None]).reshape(n_kv, grp, CHUNK, band)
    key_chunk = jnp.arange(nc)[:, None] - (w - 1) + kj[None, :] // CHUNK
    valid = key_chunk >= 0
    scores = jnp.where(valid[None, :, None, None, None, :], scores + bias[None, None], -jnp.inf)
    sink = sinks.astype(jnp.float32).reshape(n_kv, grp)[None, None, :, :, None, None]
    m = jnp.maximum(jnp.max(scores, axis=-1, keepdims=True), sink)
    p = jnp.exp(scores - m)
    probs = p / (jnp.sum(p, axis=-1, keepdims=True) + jnp.exp(sink - m))
    out = jnp.einsum('bckgqs,bcskd->bcqkgd', probs.astype(v.dtype), vb)
    return out.reshape(bsz, seq, n_h * dh)

def stick_breaking_attention(q, k, v):
    bsz, seq, n_h, dh = q.shape
    scale = dh ** -0.5
    outs = []
    for blk in range(seq // Q_BLOCK):
        lo = blk * Q_BLOCK
        hi = lo + Q_BLOCK
        z = jnp.einsum('bqhd,bshd->bhqs', q[:, lo:hi], k[:, :hi]).astype(jnp.float32) * scale
        t = lo + jnp.arange(Q_BLOCK)[:, None]
        s = jnp.arange(hi)[None, :]
        strict = s < t
        log_1mb = jnp.where(strict, jax.nn.log_sigmoid(-z), 0.0)
        after = lax.cumsum(log_1mb, axis=3, reverse=True) - log_1mb
        a = jnp.where(strict, jnp.exp(jax.nn.log_sigmoid(z) + after), 0.0)
        outs.append(jnp.einsum('bhqs,bshd->bqhd', a.astype(v.dtype), v[:, :hi]))
    return jnp.concatenate(outs, axis=1).reshape(bsz, seq, n_h * dh)

def forgetting_attention(q, k, v, log_f):
    bsz, seq, n_h, dh = q.shape
    scale = dh ** -0.5
    cum = jnp.transpose(lax.cumsum(log_f, axis=1), (0, 2, 1))
    outs = []
    for blk in range(seq // Q_BLOCK):
        lo = blk * Q_BLOCK
        hi = lo + Q_BLOCK
        z = jnp.einsum('bqhd,bshd->bhqs', q[:, lo:hi], k[:, :hi]).astype(jnp.float32) * scale
        z = z + cum[:, :, lo:hi, None] - cum[:, :, None, :hi]
        t = lo + jnp.arange(Q_BLOCK)[:, None]
        s = jnp.arange(hi)[None, :]
        p = jax.nn.softmax(jnp.where(s <= t, z, -jnp.inf), axis=-1)
        outs.append(jnp.einsum('bhqs,bshd->bqhd', p.astype(v.dtype), v[:, :hi]))
    return jnp.concatenate(outs, axis=1).reshape(bsz, seq, n_h * dh)

def memory_attention(x, mem, wq, wkv, wo):
    bsz, seq, _ = x.shape
    q = (x @ wq).reshape(bsz, seq, MEM_HEADS, MEM_HEAD_DIM)
    k, v = jnp.split((mem @ wkv).reshape(bsz, mem.shape[1], 2, MEM_HEADS, MEM_HEAD_DIM), 2, axis=2)
    k, v = k[:, :, 0], v[:, :, 0]
    s = jnp.einsum('bqhd,bmhd->bhqm', q, k).astype(jnp.float32) * (MEM_HEAD_DIM ** -0.5)
    p = jax.nn.softmax(s, axis=-1)
    o = jnp.einsum('bhqm,bmhd->bqhd', p.astype(v.dtype), v)
    return o.reshape(bsz, seq, D_MODEL) @ wo

def even_mixer(h, w_in, sinks, w_out):
    bsz, seq, _ = h.shape
    aq, ak, av, bq, bk, bv = split_cols(h @ w_in, AB_SPLITS)
    o_a = sliding_window_gqa_sinks(aq.reshape(bsz, seq, A_Q_HEADS, HEAD_DIM),
                                   ak.reshape(bsz, seq, A_KV_HEADS, HEAD_DIM),
                                   av.reshape(bsz, seq, A_KV_HEADS, HEAD_DIM), sinks)
    o_b = stick_breaking_attention(bq.reshape(bsz, seq, B_HEADS, HEAD_DIM),
                                   bk.reshape(bsz, seq, B_HEADS, HEAD_DIM),
                                   bv.reshape(bsz, seq, B_HEADS, HEAD_DIM))
    return jnp.concatenate([o_a, o_b], axis=-1) @ w_out

def odd_mixer(h, w_in, b_f, w_out):
    bsz, seq, _ = h.shape
    cq, ck, cv, cf = split_cols(h @ w_in, C_SPLITS)
    log_f = jax.nn.log_sigmoid(cf.astype(jnp.float32) + b_f.astype(jnp.float32))
    o = forgetting_attention(cq.reshape(bsz, seq, C_HEADS, HEAD_DIM),
                             ck.reshape(bsz, seq, C_HEADS, HEAD_DIM),
                             cv.reshape(bsz, seq, C_HEADS, HEAD_DIM), log_f)
    return o @ w_out

def swiglu(x, w_gate, w_up, w_down):
    return (jax.nn.silu(x @ w_gate) * (x @ w_up)) @ w_down

def moe_swiglu(x, router, w_gate, w_up, w_down):
    logits = (x @ router).astype(jnp.float32)
    top_vals, top_idx = lax.top_k(logits, TOP_K)
    gates = jax.nn.softmax(top_vals, axis=-1)
    combine = jnp.sum(jax.nn.one_hot(top_idx, N_EXPERTS, dtype=jnp.float32) * gates[..., None], axis=-2)
    y = jnp.zeros_like(x)
    for e in range(N_EXPERTS):
        y = y + combine[..., e:e + 1].astype(x.dtype) * swiglu(x, w_gate[e], w_up[e], w_down[e])
    return y

def setup_inputs(seed: int = 0) -> dict:
    key = jax.random.key(seed)
    ks = jax.random.split(key, 20)

    def nrm(k, shape, scale):
        return jax.random.normal(k, shape, jnp.float32) * scale

    d_inv = D_MODEL ** -0.5
    return {
        "x": nrm(ks[0], (BATCH, SEQ, D_MODEL), 1.0),
        "mem": nrm(ks[1], (BATCH, MEM_LEN, D_MODEL), 1.0),
        "ln_g": 1.0 + nrm(ks[2], (DEPTH, 3, D_MODEL), 0.02),
        "ln_b": nrm(ks[3], (DEPTH, 3, D_MODEL), 0.02),
        "mem_wq": nrm(ks[4], (DEPTH, D_MODEL, D_MODEL), d_inv),
        "mem_wkv": nrm(ks[5], (DEPTH, D_MODEL, 2 * D_MODEL), d_inv),
        "mem_wo": nrm(ks[6], (DEPTH, D_MODEL, D_MODEL), d_inv * BETA),
        "ab_w_in": nrm(ks[7], (N_EVEN, D_MODEL, AB_IN), d_inv),
        "ab_sinks": nrm(ks[8], (N_EVEN, A_Q_HEADS), 1.0),
        "ab_w_out": nrm(ks[9], (N_EVEN, AB_OUT, D_MODEL), AB_OUT ** -0.5 * BETA),
        "c_w_in": nrm(ks[10], (N_ODD, D_MODEL, C_IN), d_inv),
        "c_b_f": FORGET_BIAS_INIT + nrm(ks[11], (N_ODD, C_HEADS), 0.1),
        "c_w_out": nrm(ks[12], (N_ODD, C_OUT, D_MODEL), C_OUT ** -0.5 * BETA),
        "ffn_w_gate": nrm(ks[13], (N_EVEN, D_MODEL, D_FF), d_inv),
        "ffn_w_up": nrm(ks[14], (N_EVEN, D_MODEL, D_FF), d_inv),
        "ffn_w_down": nrm(ks[15], (N_EVEN, D_FF, D_MODEL), D_FF ** -0.5 * BETA),
        "moe_router": nrm(ks[16], (N_ODD, D_MODEL, N_EXPERTS), d_inv),
        "moe_w_gate": nrm(ks[17], (N_ODD, N_EXPERTS, D_MODEL, D_EXPERT), d_inv),
        "moe_w_up": nrm(ks[18], (N_ODD, N_EXPERTS, D_MODEL, D_EXPERT), d_inv),
        "moe_w_down": nrm(ks[19], (N_ODD, N_EXPERTS, D_EXPERT, D_MODEL), D_EXPERT ** -0.5 * BETA),
    }

def reference(x, mem, ln_g, ln_b, mem_wq, mem_wkv, mem_wo, ab_w_in, ab_sinks, ab_w_out,
              c_w_in, c_b_f, c_w_out, ffn_w_gate, ffn_w_up, ffn_w_down,
              moe_router, moe_w_gate, moe_w_up, moe_w_down):
    h = x
    for i in range(DEPTH):
        j = i // 2
        if i % 2 == 0:
            mix = even_mixer(h, ab_w_in[j], ab_sinks[j], ab_w_out[j])
        else:
            mix = odd_mixer(h, c_w_in[j], c_b_f[j], c_w_out[j])
        h = layer_norm(ALPHA * h + mix, ln_g[i, 0], ln_b[i, 0])
        h = layer_norm(ALPHA * h + memory_attention(h, mem, mem_wq[i], mem_wkv[i], mem_wo[i]),
                       ln_g[i, 1], ln_b[i, 1])
        if i % 2 == 0:
            ffn = swiglu(h, ffn_w_gate[j], ffn_w_up[j], ffn_w_down[j])
        else:
            ffn = moe_swiglu(h, moe_router[j], moe_w_gate[j], moe_w_up[j], moe_w_down[j])
        h = layer_norm(ALPHA * h + ffn, ln_g[i, 2], ln_b[i, 2])
    return h


_drawn_inputs = setup_inputs


def setup_inputs(seed=0):
    import zlib

    import numpy as np

    out = dict(_drawn_inputs(seed))
    spreads = {}
    factors = {'ab_sinks': 7.991, 'c_b_f': 44.04}
    for name, (base, spread) in spreads.items():
        noise = np.random.default_rng([zlib.crc32(name.encode()), seed]).standard_normal(out[name].shape)
        drawn = base * np.exp(spread * noise) if base else spread * noise
        out[name] = __import__('jax').numpy.asarray(drawn.astype(out[name].dtype))
    for name, factor in factors.items():
        out[name] = (out[name] * factor).astype(out[name].dtype)
    return out
```

```python
import concourse.bass as bass
from concourse import mybir
from contextlib import ExitStack

F32 = mybir.dt.float32
F32R = mybir.dt.float32r
I32 = mybir.dt.int32
U32 = mybir.dt.uint32
ALU = mybir.AluOpType
ACT = mybir.ActivationFunctionType
AX_X = mybir.AxisListType.X

P = 128
BIG = 1e30
LN_EPS = 1e-5


def trunk(nc, x, mem, ln_g, ln_b, mem_wq, mem_wkv, mem_wo, ab_w_in, ab_sinks, ab_w_out,
          c_w_in, c_b_f, c_w_out, ffn_w_gate, ffn_w_up, ffn_w_down,
          moe_router, moe_w_gate, moe_w_up, moe_w_down, out):
    _, SEQ, D = x.shape
    DEPTH = ln_g.shape[0]
    TB = SEQ // P
    KT = D // P
    DH = 64
    AH = ab_sinks.shape[1]
    KVH = AH // 4
    BH = D // (2 * DH)
    CH = D // DH
    MH = 4
    MDH = D // MH
    DFF = ffn_w_gate.shape[2]
    NE = moe_router.shape[2]
    DE = moe_w_gate.shape[3]
    W = 512
    ALPHA = (2.0 * DEPTH) ** 0.25
    assert (SEQ, D, TB, KT, NE, MEM_LEN := mem.shape[1]) == (256, 1024, 2, 8, 8, 256)
    SC = DH ** -0.5
    MSC = MDH ** -0.5
    TRI = 3 * P

    CK = 4
    chunks = []
    blocks = {}

    def add_block(name, w, col, cols, ck=CK):
        rows = w.shape[0] // P
        sizes = [min(ck, rows - k) for k in range(0, rows, ck)]
        blocks[name] = (len(chunks), sizes, cols)
        k = 0
        for n in sizes:
            src = w[k * P:(k + n) * P, col:col + cols].rearrange("(k p) c -> p k c", p=P)
            chunks.append((src, n, cols))
            k += n

    FB = [(j * W, min(W, DFF - j * W)) for j in range((DFF + W - 1) // W)]
    AQ, BQ = AH * DH, AH * DH + 2 * KVH * DH
    QKV = [[("q0", 0, W, CK), ("akv", AQ, 2 * KVH * DH, 8), ("bq", BQ, W, CK), ("bk", BQ + W, W, CK),
            ("bv", BQ + 2 * W, W, CK)],
           [("q0", 0, W, CK), ("q1", W, W, CK), ("k0", 2 * W, W, CK), ("k1", 3 * W, W, CK),
            ("v0", 4 * W, W, CK), ("v1", 5 * W, W, CK)]]
    for l in range(2):
        w_in = ab_w_in[0] if l == 0 else c_w_in[0]
        for name, col, cols, ck in QKV[l]:
            add_block(f"{l}{name}", w_in, col, cols, ck)
        for i in range(4):
            add_block(f"{l}kv{i}", mem_wkv[l], i * W, W)
        for i in range(2):
            add_block(f"{l}out{i}", ab_w_out[0] if l == 0 else c_w_out[0], i * W, W)
        for i in range(2):
            add_block(f"{l}mq{i}", mem_wq[l], i * W, W)
        for i in range(2):
            add_block(f"{l}mw{i}", mem_wo[l], i * W, W)
        if l == 0:
            for j, (c, n) in enumerate(FB):
                add_block(f"0g{j}", ffn_w_gate[0], c, n)
                add_block(f"0u{j}", ffn_w_up[0], c, n)
            for i in range(2):
                add_block(f"0dn{i}", ffn_w_down[0], i * W, W)
    N0 = len(chunks)
    EJ = DE // W
    EK = DE // P
    EC = 2 * 2 * EJ + 2 * (EK // CK)
    NRAW, NSPL = 6, 3
    assert EC % NRAW == 0 and EC % NSPL == 0
    CHUNK = CK * W

    with ExitStack() as ctx:
        arena_bytes = 207 * 1024 + 640
        ctx.enter_context(nc.sbuf_tensor("arena", [P, arena_bytes // 4], F32))
        START = ((nc.sbuf_base - arena_bytes) + 31) // 32 * 32
        top = [START]

        def at(name, shape, dt, off):
            size = 4
            for s in shape[1:]:
                size *= s
            assert off % 32 == 0 and off + size <= START + arena_bytes, (name, off, size)
            return nc.alloc_sbuf_tensor_at(name, shape, dt, offset=off)

        def take(name, shape, dt=F32):
            size = 4
            for s in shape[1:]:
                size *= s
            off = top[0]
            top[0] += (size + 31) // 32 * 32
            return at(name, shape, dt, off)

        raw = [take(f"raw{i}", [P, CHUNK]) for i in range(NRAW)]
        w_hi = [take(f"w_hi{i}", [P, CHUNK], F32R) for i in range(NSPL)]
        w_lo = [take(f"w_lo{i}", [P, CHUNK], F32R) for i in range(NSPL)]
        X = take("X", [P, TB, D])
        o_xt = top[0]
        xT_hi = take("xT_hi", [P, KT, SEQ], F32R)
        xT_lo = take("xT_lo", [P, KT, SEQ], F32R)
        o_mt = top[0]
        mT_hi = take("mT_hi", [P, KT, SEQ], F32R)
        mT_lo = take("mT_lo", [P, KT, SEQ], F32R)
        o_v = top[0]
        V = take("V", [P, TB, D])
        o_region = top[0]
        QK = take("QK", [P, 16, SEQ])
        o_mk = top[0]
        MK = take("MK", [P, KT, SEQ])
        MV = take("MV", [P, TB, D])
        o_o = top[0]
        O = take("O", [P, TB, D])
        o_mask = top[0]
        take("mask_room", [P, 5 * 256])
        o_scr = top[0]
        scratch = take("scratch", [P, 6 * W])
        ident = take("ident", [P, P])
        ones = take("ones", [P, P])
        tri_ge = take("tri_ge", [P, P])
        tri_lt = take("tri_lt", [P, P])
        stats = take("stats", [P, TB, 2, 6])
        mean_var = take("mean_var", [P, TB, 2])
        rstd = take("rstd", [P, TB])
        var_eps = take("var_eps", [P, TB])
        newton = take("newton", [P, TB])
        row_max = take("row_max", [P, 2, TB])
        neg_max = take("neg_max", [P, 2, TB])
        row_sum = take("row_sum", [P, 2, TB, 4])
        sink_exp = take("sink_exp", [P, 2, TB, 4])
        row_inv = take("row_inv", [P, TB, 4])
        sinks = take("sinks", [P, AH])
        neg_sinks = take("neg_sinks", [P, AH])
        gate_b = take("gate_b", [P, CH])
        f_w = take("f_w", [P, KT, CH])
        f_hi = take("f_hi", [P, KT, CH], F32R)
        f_lo = take("f_lo", [P, KT, CH], F32R)
        softp = take("softp", [P, TB, CH])
        softp_t = take("softp_t", [P, TB, CH])
        mem_tok = at("mem_tok", [P, TB, D], F32, o_mk)
        stage = at("stage", [P, 2, TB, W], F32, o_o)
        m_stage = at("m_stage", [P, TB, W], F32, o_xt)
        gb = at("gb", [P, 2, D], F32, o_v)
        dist = at("dist", [P, TRI], F32, o_mask)
        b_add = at("b_add", [P, TRI], F32, o_mask + 4 * TRI)
        b_neg8 = at("b_neg8", [P, TRI], F32, o_mask + 8 * TRI)
        c_add = at("c_add", [P, TRI], F32, o_mask)
        tri_le = at("tri_le", [P, TRI], F32, o_mask + 4 * TRI)
        f_col = at("f_col", [P, 2, TB, P], F32, o_mask + 8 * TRI)
        S_t = [at(f"S{i}", [P, W], F32, o_scr + 4 * W * i) for i in range(2)]
        P_t = [at(f"P{i}", [P, W], F32, o_scr + 4 * W * (2 + i)) for i in range(2)]
        PT_t = [at(f"PT{i}", [P, W], F32, o_scr + 4 * W * (4 + i)) for i in range(2)]
        FK = DFF // P
        hT_hi = at("hT_hi", [P, FK, SEQ], F32R, o_region)
        hT_lo = at("hT_lo", [P, FK, SEQ], F32R, o_region + 4 * FK * SEQ)
        act_g = at("act_g", [P, TB, W], F32, o_scr)
        h_tok = [at(f"h_tok{i}", [P, TB, W], F32, o_scr + 4 * TB * W * (1 + i)) for i in range(2)]
        eT_hi = at("eT_hi", [P, EK, P], F32R, o_region)
        eT_lo = at("eT_lo", [P, EK, P], F32R, o_region + 4 * EK * P)
        o = o_region + 8 * EK * P
        y_hi = at("y_hi", [P, D], F32R, o)
        y_lo = at("y_lo", [P, D], F32R, o + 4 * D)
        e_g = [at(f"e_g{i}", [P, W], F32, o + 8 * D + 4 * W * i) for i in range(2)]
        xr_hi = at("xr_hi", [P, TB, D], F32R, o_mt)
        xr_lo = at("xr_lo", [P, TB, D], F32R, o_mt + 4 * TB * D)
        xe_hi = at("xe_hi", [P, KT, P], F32R, o_xt)
        xe_lo = at("xe_lo", [P, KT, P], F32R, o_xt + 4 * KT * P)
        e_h = [at(f"e_h{i}", [P, W], F32, o_scr + 4 * W * i) for i in range(2)]
        pick = at("pick", [P, TB, P], F32R, o_scr + 8 * W)
        pickT = at("pickT", [P, TB, P], F32R, o_scr + 8 * W + 4 * TB * P)
        o = o_scr + 8 * W + 8 * TB * P
        slot_no = at("slot_no", [P, P], F32, o)
        o += 4 * P
        r_w = at("r_w", [P, KT, NE], F32, o)
        r_hi = at("r_hi", [P, KT, NE], F32R, o + 256)
        r_lo = at("r_lo", [P, KT, NE], F32R, o + 512)
        o += 768
        small = {}
        for name, shape, dt in (
                ("logit", [P, TB, NE], F32), ("best", [P, TB, 8], F32), ("best_i", [P, TB, 8], U32),
                ("best_f", [P, TB, 8], F32), ("hot1", [P, TB, NE], F32), ("hot2", [P, TB, NE], F32),
                ("gap", [P, TB], F32), ("g1", [P, TB], F32), ("g2", [P, TB], F32),
                ("taken", [P, TB, NE], F32), ("wt", [P, TB, 3 * NE], F32),
                ("place", [P, TB, 3 * NE], F32), ("most", [P, 1], F32), ("rounds", [P, 1], I32),
                ("slot_w", [P, 1], F32)):
            small[name] = at(name, shape, dt, o)
            size = 4
            for s in shape[1:]:
                size *= s
            o += (size + 31) // 32 * 32
        assert o <= o_scr + 4 * 6 * W, o - o_scr
        logit, best, best_i, best_f = (small[n] for n in ("logit", "best", "best_i", "best_f"))
        hot1, hot2, gap, g1, g2 = (small[n] for n in ("hot1", "hot2", "gap", "g1", "g2"))
        taken, wt, place, most, rounds, slot_w = (
            small[n] for n in ("taken", "wt", "place", "most", "rounds", "slot_w"))

        bank = [ctx.enter_context(nc.psum_tensor(f"bank{i}", [P, W], F32)) for i in range(8)]

        sems = {}

        def sem(name):
            if name not in sems:
                sems[name] = ctx.enter_context(nc.semaphore(name))
            return sems[name]

        raw_in = [sem(f"raw_in{i}") for i in range(NRAW)]
        hi_made = sem("hi_made")
        lo_made = sem("lo_made")
        chunk_used = sem("chunk_used")
        filled = [sem(f"filled{i}") for i in range(8)]
        emptied = [sem(f"emptied{i}") for i in range(8)]

        fillings = {}
        claims = [0] * 8
        signals = [0] * 8
        JOB_CLAIMS = [5, 5, 5, 4, 2, 2, 5, 4]
        JOB_SIGNALS = [1, 2, 1, 1, 1, 1, 5, 4]

        def claim(eng, key, b, job=None, signal=True, wait=True):
            if claims[b] and wait:
                eng.wait_ge(emptied[b], claims[b] + (0 if job is None else JOB_CLAIMS[b] * job))
            claims[b] += 1
            signals[b] += signal
            fillings[key] = (b, claims[b], signals[b])
            return bank[b]

        def wait_filled(eng, key, job=None):
            b, _, n = fillings[key]
            eng.wait_ge(filled[b], n + (0 if job is None else JOB_SIGNALS[b] * job))
            return bank[b]

        def wait_emptied(eng, key, job=None):
            b, n, _ = fillings[key]
            eng.wait_ge(emptied[b], n + (0 if job is None else JOB_CLAIMS[b] * job))

        def bank_of(key):
            return bank[fillings[key][0]]

        def empties(ins, key):
            ins.then_inc(emptied[fillings[key][0]], 1)

        def last_chunk(name):
            return blocks[name][0] + len(blocks[name][1]) - 1

        def wait_block(eng, name):
            eng.wait_ge(chunk_used, last_chunk(name) + 1)

        block = ctx.enter_context(nc.Block())

        def units(l):
            if l == 1:
                return [("C", h // 2, 8 + h // 2, 64 * (h % 2), h * DH, h) for h in range(CH)]
            a = [("A", h // 2, 4 + h // 4, 64 * (h % 2), (h // 4) * DH, h) for h in range(AH)]
            b = [("B", 6 + h // 2, 10 + h // 2, 64 * (h % 2), P + h * DH, h) for h in range(BH)]
            return a + b

        NU = 16
        TILES = [{"q0": 0, "akv": 4, "bq": 6, "bk": 10}, {"q0": 0, "q1": 4, "k0": 8, "k1": 12}]
        VALUES = [{"bv": P}, {"v0": 0, "v1": W}]
        LNS = [(l, i) for l in range(2) for i in range(3)]

        @block.tensor
        def _(pe):
            pair = [0]

            def chunk_product(c, outs, lhs_hi, lhs_lo, k0, first, last, cols, idx=None, slot=None,
                              rows=None, done=None, ready=None):
                n = chunks[c][1] if idx is None else CK
                pe.wait_ge(lo_made, c + 1 if idx is None else idx + 1)
                s = c % NSPL if slot is None else slot
                hi = w_hi[s][:, 0:n * cols].rearrange("p (k c) -> p k c", k=n)
                lo = w_lo[s][:, 0:n * cols].rearrange("p (k c) -> p k c", k=n)
                for k in rows or range(n):
                    if ready and (k0 + k) % 2 == 0:
                        wait_emptied(pe, f"{ready}.{(k0 + k) // 2}")
                    for t, dst in outs:
                        xh = lhs_hi[:, k0 + k, t * P:(t + 1) * P]
                        xl = lhs_lo[:, k0 + k, t * P:(t + 1) * P]
                        d = dst[:, 0:cols]
                        nc.tensor.matmul(d, xh, hi[:, k, :], start=(first and k == 0), stop=False)
                        nc.tensor.matmul(d, xh, lo[:, k, :], start=False, stop=False)
                        m = nc.tensor.matmul(d, xl, hi[:, k, :], start=False,
                                             stop=(last and k == n - 1))
                if done is not None:
                    m.then_inc(done, 1)

            def product(name, lhs_hi, lhs_lo, between=None, ready=None, split_end=False):
                c0, sizes, cols = blocks[name]
                p = pair[0] % 2
                pair[0] += 1
                outs = [(t, claim(pe, f"{name}.{t}", 2 * p + t, signal=(split_end and t == 0)))
                        for t in range(TB)]
                k0 = 0
                last = len(sizes) - 1
                for i, n in enumerate(sizes):
                    if split_end and i == last - 1:
                        for t in range(TB):
                            for j in (i, i + 1):
                                chunk_product(c0 + j, outs[t:t + 1], lhs_hi, lhs_lo,
                                              k0 + (j - i) * n, j == 0, j == last, cols, ready=ready,
                                              done=chunk_used if t else filled[2 * p] if j == last
                                              else None)
                        break
                    chunk_product(c0 + i, outs, lhs_hi, lhs_lo, k0, i == 0, i == last, cols,
                                  done=chunk_used, ready=ready)
                    k0 += n
                    if between is not None:
                        between(i)

            def transposes(key, src, tiles, b0, ready=None):
                dst = [claim(pe, f"{key}.{q // 2}", b0 + q // 2) for q in range(0, tiles, 2)]
                for t in range(TB):
                    if ready is not None:
                        pe.wait_ge(*ready[t])
                    for k in range(tiles):
                        c = (k % 2) * SEQ + t * P
                        m = nc.tensor.transpose(dst[k // 2][:, c:c + P], src[:, t, k * P:(k + 1) * P],
                                                ident[:, :])
                        if t == TB - 1 and (k % 2 or k == tiles - 1):
                            m.then_inc(filled[b0 + k // 2], 1)

            pe.wait_ge(sem("consts"), 1)
            pe.wait_ge(sem("x_in"), 16)
            transposes("0x", X, KT, 0)
            pe.wait_ge(sem("mem_in"), 16)
            transposes("m", mem_tok, KT, 4)
            ready = "0x"

            for l in range(2):
                names = [n for n, *_ in QKV[l]]
                tjob = [0]
                if l == 1:
                    pe.wait_ge(sem("f_split"), 1)
                    for q in range(4):
                        wait_emptied(pe, f"{ready}.{q}")
                    dst = claim(pe, "f", 4)
                    for k in range(KT):
                        for t in range(TB):
                            d = dst[:, t * CH:(t + 1) * CH]
                            xh, xl = (w[:, k, t * P:(t + 1) * P] for w in (xT_hi, xT_lo))
                            one = k == 0 and t == 0
                            nc.tensor.matmul(d, xh, f_hi[:, k, :], start=one, stop=False,
                                             skip_group_check=True)
                            nc.tensor.matmul(d, xh, f_lo[:, k, :], start=False, stop=False,
                                             skip_group_check=True)
                            m = nc.tensor.matmul(d, xl, f_hi[:, k, :], start=False,
                                                 stop=(k == KT - 1), skip_group_check=True)
                    m.then_inc(filled[4], 1)

                def qk_transposes(name, l=l, tjob=tjob):
                    for t in range(TB):
                        wait_emptied(pe, f"{l}{name}.{t}")
                    tiles = 2 if name == "akv" else 4
                    transposes(f"{l}{name}T", stage[:, tjob[0] % 2, :, :], tiles, 4 + 2 * (tjob[0] % 2))
                    tjob[0] += 1

                for i, name in enumerate(names):
                    before = names[i - 1] if i and names[i - 1] in TILES[l] else None
                    product(f"{l}{name}", xT_hi, xT_lo, ready=ready,
                            between=(lambda c, b=before: qk_transposes(b) if c == 0 and b else None))
                for name in names:
                    if name in TILES[l]:
                        for q in range(1 if name == "akv" else 2):
                            wait_emptied(pe, f"{l}{name}T.{q}")

                us = units(l)

                def scores(i, l=l, us=us):
                    kind, q, k, base, _, h = us[i]
                    b = 4 + i % 3
                    d = claim(pe, f"{l}s{i}", b)
                    rows = slice(base, base + DH)
                    qT, kT = QK[rows, q, :], QK[rows, k, :]
                    if kind == "B":
                        nc.tensor.matmul(d[:, 0:SEQ], kT[:, 0:P], qT, start=True, stop=False,
                                         skip_group_check=True)
                        m = nc.tensor.matmul(d[:, SEQ:TRI], kT[:, P:SEQ], qT[:, P:SEQ], start=False,
                                             stop=True, skip_group_check=True)
                    else:
                        c = kind == "C"
                        if c:
                            pe.wait_ge(sem("f_col_made"), i + 1)
                            nc.tensor.matmul(d[:, 0:TRI], f_col[:, i % 2, 0, :], tri_le[:, :],
                                             start=True, stop=False, skip_group_check=True)
                            nc.tensor.matmul(d[:, SEQ:TRI], f_col[:, i % 2, 1, :], tri_le[:, 0:P],
                                             start=False, stop=False, skip_group_check=True)
                        nc.tensor.matmul(d[:, 0:P], qT[:, 0:P], kT[:, 0:P], start=not c, stop=True,
                                         skip_group_check=True)
                        m = nc.tensor.matmul(d[:, P:TRI], qT[:, P:SEQ], kT, start=not c, stop=True,
                                             skip_group_check=True)
                    m.then_inc(filled[b], 1)

                def second(i, l=l, us=us):
                    kind = us[i][0]
                    b = 4 + i % 3
                    src = P_t[i % 2]
                    if kind == "B":
                        pe.wait_ge(sem(f"logs_made{l}"), i + 1 - AH)
                        d = claim(pe, f"{l}t{i}", b)
                        nc.tensor.matmul(d[:, 0:SEQ], tri_ge[:, :], src[:, 0:SEQ], start=False,
                                         stop=False, skip_group_check=True)
                        nc.tensor.matmul(d[:, P:SEQ], ones[:, :], src[:, SEQ:TRI], start=False,
                                         stop=False, skip_group_check=True)
                        m = nc.tensor.matmul(d[:, SEQ:TRI], tri_ge[:, :], src[:, SEQ:TRI],
                                             start=False, stop=True, skip_group_check=True)
                    else:
                        pe.wait_ge(sem(f"probs_made{l}"), 2 * (i + 1))
                        d = claim(pe, f"{l}t{i}", b)
                        for q in range(3):
                            m = nc.tensor.transpose(d[:, q * P:(q + 1) * P], src[:, q * P:(q + 1) * P],
                                                    ident[:, :])
                    m.then_inc(filled[b], 1)

                def values(i, l=l, us=us):
                    kind, vcol = us[i][0], us[i][4]
                    if kind == "B":
                        pe.wait_ge(sem(f"aT_made{l}"), i + 1 - AH)
                    else:
                        wait_emptied(pe, f"{l}t{i}")
                    if i == 0:
                        for name in names:
                            for t in range(TB if name not in TILES[l] else 0):
                                wait_emptied(pe, f"{l}{name}.{t}")
                    if i % 4 == 0:
                        claim(pe, f"{l}o{i // 4}", 7, signal=False)
                    pT = PT_t[i % 2]
                    d = bank[7][:, :].rearrange("p (t u d) -> p t u d", t=TB, u=4)[:, :, i % 4, :]
                    nc.tensor.matmul(d[:, 0, :], pT[:, 0:P], V[:, 0, vcol:vcol + DH], start=True,
                                     stop=True, skip_group_check=True)
                    nc.tensor.matmul(d[:, 1, :], pT[:, P:SEQ], V[:, 0, vcol:vcol + DH], start=True,
                                     stop=False, skip_group_check=True)
                    nc.tensor.matmul(d[:, 1, :], pT[:, SEQ:TRI], V[:, 1, vcol:vcol + DH], start=False,
                                     stop=True, skip_group_check=True).then_inc(sem(f"unit_done{l}"), 1)

                fill_outs = [None]

                def mem_kv(i, l=l, fill_outs=fill_outs):
                    if i >= NU:
                        return
                    c = i // 2
                    name = f"{l}kv{c // 2}"
                    if i % 4 == 0:
                        p = pair[0] % 2
                        pair[0] += 1
                        fill_outs[0] = [(t, claim(pe, f"{name}.{t}", 2 * p + t, signal=False))
                                        for t in range(TB)]
                    chunk_product(blocks[name][0] + c % 2, fill_outs[0], mT_hi, mT_lo, 4 * (c % 2),
                                  c % 2 == 0, c % 2 == 1, W, rows=((0, 1), (2, 3))[i % 2],
                                  done=chunk_used if i % 2 else None, ready="m")

                def mem_kT(i, l=l):
                    if i not in (5, 9):
                        return
                    name = f"{l}kv{i // 4 - 1}"
                    for t in range(TB):
                        wait_emptied(pe, f"{name}.{t}")
                    transposes(f"{name}T", m_stage, 4, 2 * (pair[0] % 2))
                    pair[0] += 1

                for i in range(NU + 2):
                    if i < NU:
                        scores(i)
                    mem_kT(i)
                    mem_kv(i)
                    if 1 <= i <= NU:
                        second(i - 1)
                    if i >= 2:
                        values(i - 2)

                def normed_T(key, n):
                    transposes(key, X, KT, 4, ready=[(sem("normed"), 2 * n + t + 1) for t in range(TB)])

                transposes(f"{l}oT", O, KT, 4, ready=[(sem(f"o_made{l}"), NU // 4)] * TB)
                for i in range(2):
                    product(f"{l}out{i}", xT_hi, xT_lo, ready=f"{l}oT", split_end=(i == 1))
                normed_T(f"{l}n0", 3 * l)

                stage_m = [f"{l}mq0", f"{l}mq1"]

                def mq_transposes(i, l=l):
                    for t in range(TB):
                        wait_emptied(pe, f"{l}mq{i}.{t}")
                    transposes(f"{l}mq{i}T", stage[:, i, :, :], 4, 4 + 2 * i)

                product(stage_m[0], xT_hi, xT_lo, ready=f"{l}n0")
                product(stage_m[1], xT_hi, xT_lo, between=lambda c: mq_transposes(0) if c == 0 else None)
                mq_transposes(1)
                for q in range(2):
                    for name in stage_m:
                        wait_emptied(pe, f"{name}T.{q}")
                for h in range(MH + 2):
                    if h < MH:
                        b = 4 + h % 3
                        d = claim(pe, f"{l}ms{h}", b)
                        for t in range(TB):
                            for k in range(2):
                                m = nc.tensor.matmul(d[:, t * SEQ:(t + 1) * SEQ],
                                                     QK[:, 2 * h + k, t * P:(t + 1) * P],
                                                     MK[:, 2 * h + k, :], start=(k == 0), stop=(k == 1))
                        m.then_inc(filled[b], 1)
                    if 1 <= h <= MH:
                        i, b = h - 1, 4 + (h - 1) % 3
                        pe.wait_ge(sem(f"m_probs_made{l}"), 2 * (i + 1))
                        d = claim(pe, f"{l}mt{i}", b)
                        for mb in range(2):
                            for t in range(TB):
                                m = nc.tensor.transpose(
                                    d[:, mb * SEQ + t * P:mb * SEQ + (t + 1) * P],
                                    P_t[i % 2][:, t * SEQ + mb * P:t * SEQ + (mb + 1) * P], ident[:, :])
                        m.then_inc(filled[b], 1)
                    if h >= 2:
                        i = h - 2
                        b = 2 + i % 2
                        wait_emptied(pe, f"{l}mt{i}")
                        d = claim(pe, f"{l}mo{i}", b)
                        for t in range(TB):
                            for mb in range(2):
                                m = nc.tensor.matmul(
                                    d[:, t * MDH:(t + 1) * MDH],
                                    PT_t[i % 2][:, mb * SEQ + t * P:mb * SEQ + (t + 1) * P],
                                    MV[:, mb, i * MDH:(i + 1) * MDH], start=(mb == 0), stop=(mb == 1))
                        m.then_inc(filled[b], 1)
                for i in range(MH):
                    wait_emptied(pe, f"{l}mo{i}")
                transposes(f"{l}moT", O, KT, 4)
                for i in range(2):
                    product(f"{l}mw{i}", xT_hi, xT_lo, ready=f"{l}moT", split_end=(i == 1))
                normed_T(f"{l}n1", 3 * l + 1)
                ready = f"{l}n1"

                if l == 0:
                    def h_transposes(j):
                        for t in range(TB):
                            wait_emptied(pe, f"0u{j}.{t}")
                        transposes(f"0h{j}T", h_tok[j % 2], FB[j][1] // P, 4 + 2 * (j % 2))

                    for j in range(len(FB)):
                        product(f"0g{j}", xT_hi, xT_lo, ready=ready,
                                between=(lambda c, j=j: h_transposes(j - 1) if c == 0 and j else None))
                        product(f"0u{j}", xT_hi, xT_lo)

                    def down_between(i, c):
                        if i == 0 and c == 0:
                            h_transposes(len(FB) - 1)
                        if i == 0 and c == 3:
                            for j in range(len(FB)):
                                for q in range(FB[j][1] // (2 * P)):
                                    wait_emptied(pe, f"0h{j}T.{q}")

                    for j in range(len(FB) - 1):
                        for q in range(2):
                            if j < len(FB) - 2:
                                wait_emptied(pe, f"0h{j}T.{q}")
                    for i in range(2):
                        product(f"0dn{i}", hT_hi, hT_lo, between=lambda c, i=i: down_between(i, c),
                                split_end=(i == 1))
                    normed_T("0n2", 2)
                    ready = "0n2"

            pe.wait_ge(sem("r_split"), 1)
            for q in range(4):
                wait_emptied(pe, f"{ready}.{q}")
            d = claim(pe, "router", 4)
            for k in range(KT):
                for t in range(TB):
                    o_ = d[:, t * NE:(t + 1) * NE]
                    xh, xl = (w[:, k, t * P:(t + 1) * P] for w in (xT_hi, xT_lo))
                    nc.tensor.matmul(o_, xh, r_hi[:, k, :], start=(k == 0 and t == 0), stop=False,
                                     skip_group_check=True)
                    nc.tensor.matmul(o_, xh, r_lo[:, k, :], start=False, stop=False,
                                     skip_group_check=True)
                    m = nc.tensor.matmul(o_, xl, r_hi[:, k, :], start=False, stop=(k == KT - 1),
                                         skip_group_check=True)
            m.then_inc(filled[4], 1)
            pe.wait_ge(sem("taken_made"), 1)
            d = claim(pe, "places", 5)
            nc.tensor.matmul(d[:, 0:NE], tri_lt[:, :], taken[:, 0, :], start=True, stop=True,
                             skip_group_check=True)
            nc.tensor.matmul(d[:, NE:2 * NE], ones[:, :], taken[:, 0, :], start=True, stop=False,
                             skip_group_check=True)
            nc.tensor.matmul(d[:, NE:2 * NE], tri_lt[:, :], taken[:, 1, :], start=False, stop=True,
                             skip_group_check=True)
            for t in range(TB):
                m = nc.tensor.matmul(d[:, 2 * NE:3 * NE], ones[:, :], taken[:, t, :], start=(t == 0),
                                     stop=(t == 1), skip_group_check=True)
            m.then_inc(filled[5], 1)

            def gather(tag, job):
                for part, src in enumerate((xr_hi, xr_lo)):
                    for half in range(2):
                        b = 2 * part + half
                        d = claim(pe, f"{tag}{b}", b, job)
                        for kk in range(4):
                            k = 4 * half + kk
                            for t in range(TB):
                                m = nc.tensor.matmul(d[:, kk * P:(kk + 1) * P],
                                                     src[:, t, k * P:(k + 1) * P], pick[:, t, :],
                                                     start=(t == 0), stop=(t == 1))
                        m.then_inc(filled[b], 1)

            def slots(tag, job, nxt):
                d = claim(pe, tag, 1, job)
                for t in range(TB):
                    nc.tensor.transpose(d[:, t * P:(t + 1) * P], pick[:, t, :].bitcast(F32), ident[:, :])
                for t in range(TB):
                    m = nc.tensor.matmul(d[:, 2 * P:2 * P + 1], pick[:, t, :].bitcast(F32),
                                         wt[:, t, nxt], start=(t == 0), stop=(t == 1),
                                         skip_group_check=True)
                m.then_inc(filled[1], 1)

            pe.wait_ge(sem("xr_made"), 2)
            pe.wait_ge(sem("picked"), 1)
            gather("gA", None)
            pe.wait_ge(sem("gates_made"), 1)
            slots("pA", None, slice(0, 1))
            pe.wait_ge(sem("rounds_made"), 1)
            n_rounds = pe.value_load(rounds[0:1, 0:1], min_val=1, max_val=2)
            before = [list(claims), list(signals)]
            with pe.Fori(0, n_rounds * NE) as job:
                for b in range(4):
                    pe.wait_ge(emptied[b], claims[b] - (1 if b == 1 else 0) + JOB_CLAIMS[b] * job)
                for c in range(EC):
                    idx = N0 + c + EC * job
                    if c < 4 * EJ:
                        j, q = c // 4, c % 4
                        key, b = (f"eg{j}", j % 2) if q < 2 else (f"eu{j}", 2 + j % 2)
                        if q % 2 == 0:
                            claim(pe, key, b, job, signal=False)
                        chunk_product(c, [(0, bank[b])], xe_hi, xe_lo, 4 * (q % 2), q % 2 == 0,
                                      q % 2 == 1, W, idx=idx, slot=(N0 + c) % NSPL, done=chunk_used)
                    else:
                        i, q = divmod(c - 4 * EJ, EK // CK)
                        if q == 0:
                            claim(pe, f"ed{i}", 4 + i, job, signal=False)
                        if i == 0:
                            wait_emptied(pe, f"et{q}", job)
                        chunk_product(c, [(0, bank[4 + i])], eT_hi, eT_lo, CK * q, q == 0,
                                      q == EK // CK - 1, W, idx=idx, slot=(N0 + c) % NSPL,
                                      done=chunk_used)
                    if c % 4 == 1 and 1 <= c // 4 <= EJ:
                        j = c // 4 - 1
                        b = 6 + j % 2
                        pe.wait_ge(sem("e_hidden"), EJ * job + j + 1)
                        d = claim(pe, f"et{j}", b, job)
                        for q in range(4):
                            m = nc.tensor.transpose(d[:, q * P:(q + 1) * P],
                                                    e_h[j % 2][:, q * P:(q + 1) * P], ident[:, :])
                        m.then_inc(filled[b], 1)
                pe.wait_ge(sem("picked"), job + 2)
                gather("gB", job)
                for i in range(2):
                    wait_emptied(pe, f"ed{i}", job)
                    for t in range(TB):
                        b = (6 + t) if i == 0 else (4 + t)
                        d = claim(pe, f"ec{i}{t}", b, job)
                        nc.tensor.matmul(d[:, :], pickT[:, t, :], y_hi[:, i * W:(i + 1) * W],
                                         start=True, stop=False)
                        nc.tensor.matmul(d[:, :], pickT[:, t, :], y_lo[:, i * W:(i + 1) * W],
                                         start=False, stop=True).then_inc(filled[b], 1)
                slots("pB", job, bass.ds(job + 1, 1))
            assert [a - b for a, b in zip(claims, before[0])] == JOB_CLAIMS
            assert [a - b for a, b in zip(signals, before[1])] == JOB_SIGNALS

        @block.sync
        def _(sp):
            sp.dma_start(X[:, :, :], x[0].rearrange("(t p) d -> p t d", p=P)).then_inc(sem("x_in"), 16)
            for c, (src, n, cols) in enumerate(chunks):
                if c >= NRAW:
                    sp.wait_ge(lo_made, c - NRAW + 1)
                dst = raw[c % NRAW][:, 0:n * cols].rearrange("p (k c) -> p k c", k=n)
                sp.dma_start(dst, src).then_inc(raw_in[c % NRAW], 16)

            def expert_chunks(e, job):
                for c in range(EC):
                    sp.wait_ge(lo_made, N0 + c - NRAW + 1 + EC * job)
                    if c < 4 * EJ:
                        j, q = c // 4, c % 4
                        w = moe_w_gate if q < 2 else moe_w_up
                        k0, col = CK * (q % 2), j * W
                    else:
                        i, q = divmod(c - 4 * EJ, EK // CK)
                        w, k0, col = moe_w_down, CK * q, i * W
                    src = w[0][bass.ds(e, 1), k0 * P:(k0 + CK) * P, col:col + W].rearrange(
                        "e (k p) c -> p (e k) c", p=P)
                    s = (N0 + c) % NRAW
                    sp.dma_start(raw[s][:, :].rearrange("p (k c) -> p k c", k=CK), src)\
                      .then_inc(raw_in[s], 16)

            with sp.Fori(0, NE) as e:
                expert_chunks(e, e)
            sp.wait_ge(sem("rounds_made"), 1)
            n_rounds = sp.value_load(rounds[0:1, 0:1], min_val=1, max_val=2)
            with sp.If(n_rounds > 1):
                with sp.Fori(0, NE) as e:
                    expert_chunks(e, e + NE)
            with sp.Else():
                sp.nop()
            for t in range(TB):
                sp.wait_ge(sem("normed"), 2 * 5 + t + 1)
                sp.dma_start(out[0].rearrange("(t p) d -> p t d", p=P)[:, t, :], X[:, t, :])\
                  .then_inc(sem("out_done"), 16)
            sp.wait_ge(sem("out_done"), 16 * TB)

        @block.gpsimd
        def _(pool):
            def mask(dst, width, base, step, cm, fill, op=ALU.is_ge):
                return nc.gpsimd.affine_select(out=dst, in_=dst, pattern=[[step, width]],
                                               compare_op=op, fill=fill, base=base,
                                               channel_multiplier=cm)

            chain = [0]

            def link(ins):
                chain[0] += 1
                ins.then_inc(sem("pool_chain"), 1)
                pool.wait_ge(sem("pool_chain"), chain[0])

            pool.dma_start(mem_tok[:, :, :], mem[0].rearrange("(t p) d -> p t d", p=P))\
                .then_inc(sem("mem_in"), 16)
            pool.dma_start(sinks[:, :], ab_sinks[0].partition_broadcast(P)).then_inc(sem("sink_in"), 16)
            pool.dma_start(gate_b[:, :], c_b_f[0].partition_broadcast(P)).then_inc(sem("b_in"), 16)
            pool.dma_start(f_w[:, :, :], c_w_in[0][:, 3 * D:3 * D + CH].rearrange("(k p) c -> p k c", p=P))\
                .then_inc(sem("f_in"), 16)
            link(nc.gpsimd.memset(ident[:, :], 0.0))
            link(mask(ident[:, :], P, 0, -1, 1, 1.0, ALU.not_equal))
            link(nc.gpsimd.memset(ones[:, :], 1.0))
            link(nc.gpsimd.memset(tri_ge[:, :], 1.0))
            link(mask(tri_ge[:, :], P, 0, -1, 1, 0.0))
            link(nc.gpsimd.memset(tri_lt[:, :], 1.0))
            mask(tri_lt[:, :], P, -1, 1, -1, 0.0).then_inc(sem("consts"), 1)
            link(nc.gpsimd.iota(dist[:, 0:P], [[-1, P]], base=0, channel_multiplier=1,
                                allow_small_or_imprecise_dtypes=True))
            link(nc.gpsimd.iota(dist[:, P:TRI], [[-1, SEQ]], base=P, channel_multiplier=1,
                                allow_small_or_imprecise_dtypes=True))
            link(nc.gpsimd.memset(b_add[:, :], 0.0))
            link(mask(b_add[:, 0:P], P, -1, 1, -1, -BIG))
            link(mask(b_add[:, SEQ:TRI], P, -1, 1, -1, -BIG))
            link(nc.gpsimd.memset(b_neg8[:, :], -1.0 / SC))
            link(mask(b_neg8[:, 0:P], P, -1, 1, -1, 0.0))
            link(mask(b_neg8[:, SEQ:TRI], P, -1, 1, -1, 0.0))
            nc.gpsimd.nop().then_inc(sem("masks0"), 1)
            pool.wait_ge(sem("dist_abs"), 1)
            link(mask(dist[:, 64:P], 64, -64, 0, 1, BIG))
            link(nc.gpsimd.memset(dist[:, P:P + 64], BIG))
            link(mask(dist[:, P + 64:SEQ], 64, 63, 0, -1, BIG))
            mask(dist[:, SEQ + 64:TRI], 64, -64, 0, 1, BIG).then_inc(sem("masks0"), 1)

            def ln_params(n):
                l, i = LNS[n]
                if i == 0:
                    pool.wait_ge(sem(f"unit_done{l}"), NU)
                else:
                    pool.wait_ge(sem("normed"), 2 * n)
                pool.dma_start(gb[:, 0, :], ln_g[l, i].partition_broadcast(P)).then_inc(sem("ln_in"), 16)
                pool.dma_start(gb[:, 1, :], ln_b[l, i].partition_broadcast(P)).then_inc(sem("ln_in"), 16)
                pool.wait_ge(sem("ln_in"), 32 * (n + 1))

            for n in range(3):
                ln_params(n)
            wait_block(pool, "0dn1")
            link(nc.gpsimd.memset(c_add[:, :], 0.0))
            link(mask(c_add[:, 0:P], P, 0, -1, 1, -BIG))
            link(mask(c_add[:, SEQ:TRI], P, 0, -1, 1, -BIG))
            link(nc.gpsimd.memset(tri_le[:, :], 1.0))
            link(mask(tri_le[:, 0:P], P, 0, 1, -1, 0.0))
            mask(tri_le[:, P:SEQ], P, 0, 1, -1, 0.0).then_inc(sem("masks1"), 1)
            pool.wait_ge(sem("masks1"), 1)
            pool.wait_ge(sem("softp_made"), 1)
            for i in range(CH):
                if i >= 2:
                    wait_filled(pool, f"1s{i - 2}")
                for t in range(TB):
                    ins = nc.gpsimd.tensor_scalar(f_col[:, i % 2, t, :], ones[:, :],
                                                  softp[:, t, i:i + 1], None, ALU.mult)
                    if t == 0:
                        link(ins)
                ins.then_inc(sem("f_col_made"), 1)
            ln_params(3)
            ln_params(4)
            for i in range(MH):
                wait_filled(pool, f"1mo{i}")
            pool.dma_start(r_w[:, :, :], moe_router[0].rearrange("(k p) e -> p k e", p=P))\
                .then_inc(sem("r_in"), 16)
            nc.gpsimd.iota(slot_no[:, :], [[1, P]], base=1, channel_multiplier=0,
                           allow_small_or_imprecise_dtypes=True).then_inc(sem("slot_made"), 1)
            ln_params(5)

        @block.scalar
        def _(act):
            cursor = [0]

            def copy(dst, src):
                return nc.scalar.activation(dst, src, ACT.Copy)

            def split(upto):
                while cursor[0] <= min(upto, N0 + NSPL - 1):
                    c = cursor[0]
                    cursor[0] += 1
                    if c >= N0:
                        n = CHUNK
                    else:
                        n = chunks[c][1] * chunks[c][2]
                    act.wait_ge(raw_in[c % NRAW], 16 * (c // NRAW + 1))
                    if c >= NSPL:
                        act.wait_ge(chunk_used, c - NSPL + 1)
                    copy(w_hi[c % NSPL][:, 0:n], raw[c % NRAW][:, 0:n]).then_inc(hi_made, 1)

            def split_to(key, hi):
                for q in range(4):
                    b = wait_filled(act, f"{key}.{q}")
                    copy(hi[:, 2 * q:2 * q + 2, :].rearrange("p k t -> p (k t)"), b[:, :])\
                        .then_inc(sem("t_hi"), 1)

            def start_rstd(n):
                for t in range(TB):
                    r = rstd[:, t:t + 1]
                    act.wait_ge(sem("var_made"), 2 * n + t + 1)
                    nc.scalar.activation(r, var_eps[:, t:t + 1], ACT.Ln).then_inc(sem("var_ln"), 1)
                    act.wait_ge(sem("var_ln"), 2 * n + t + 1)
                    nc.scalar.activation(r, r, ACT.Exp, scale=-0.5).then_inc(sem("rstd_made"), 1)

            def last_block(name):
                split(last_chunk(name) + 1)

            def after(name):
                split(last_chunk(name) + NSPL - 1)
                wait_block(act, name)

            split_to("0x", xT_hi)
            split(NSPL - 1)
            split_to("m", mT_hi)
            for l in range(2):
                names = [n for n, *_ in QKV[l]]
                if l == 1:
                    act.wait_ge(sem("fu_made"), 1)
                    nc.scalar.activation(softp_t[:, :, :], softp_t[:, :, :], ACT.Exp)\
                        .then_inc(sem("act_chain"), 1)
                    act.wait_ge(sem("act_chain"), 1)
                    nc.scalar.activation(softp_t[:, :, :], softp_t[:, :, :], ACT.Ln, bias=1.0)\
                        .then_inc(sem("fl_made"), 1)

                def qk_evacuate(name, l=l):
                    b = wait_filled(act, f"{l}{name}T.0")
                    t0 = TILES[l][name]
                    empties(copy(QK[:, t0:t0 + 2, :].rearrange("p k t -> p (k t)"), b[:, :]),
                            f"{l}{name}T.0")

                for i, name in enumerate(names):
                    if i and names[i - 1] in TILES[l]:
                        split(blocks[f"{l}{name}"][0] + NSPL - 1)
                        qk_evacuate(names[i - 1])
                    after(f"{l}{name}")
                    key = f"{l}{name}.0"
                    src = bank_of(key)
                    if name in TILES[l]:
                        back = [n for n in names[:i] if n in TILES[l]]
                        if len(back) >= 2:
                            for q in range(1 if back[-2] == "akv" else 2):
                                wait_filled(act, f"{l}{back[-2]}T.{q}")
                        dst = stage[:, len(back) % 2, 0, :]
                    if name == "akv":
                        kv = dst[:, 0:2 * P].rearrange("p (h r d) -> p h r d", h=KVH, r=2)
                        s = src[:, 0:P].rearrange("p (h d) -> p h d", h=KVH)
                        copy(kv[:, :, 0, :], s)
                        copy(kv[:, :, 1, :], s)
                        empties(copy(V[:, 0, 0:P], src[:, P:2 * P]), key)
                    elif name in TILES[l]:
                        empties(copy(dst, src[:, :]), key)
                    else:
                        v0 = VALUES[l][name]
                        empties(copy(V[:, 0, v0:v0 + W], src[:, :]), key)
                us = units(l)

                def first(i, l=l, us=us):
                    kind = us[i][0]
                    S, Pb = S_t[i % 2], P_t[i % 2]
                    if kind == "B":
                        j = i - AH
                        act.wait_ge(sem(f"zc_made{l}"), j + 1)
                        nc.scalar.activation(S[:, 0:TRI], S[:, 0:TRI], ACT.Exp).then_inc(sem(f"ez{l}"), 1)
                        act.wait_ge(sem(f"ez{l}"), j + 1)
                        nc.scalar.activation(S[:, 0:TRI], S[:, 0:TRI], ACT.Ln, bias=1.0)\
                            .then_inc(sem(f"lnz_made{l}"), 1)
                        return
                    act.wait_ge(sem(f"max_made{l}"), i + 1)
                    if i >= 2:
                        wait_filled(act, f"{l}t{i - 2}")
                    for t, (a, b) in enumerate(((0, P), (P, TRI))):
                        nc.scalar.activation(Pb[:, a:b], S[:, a:b], ACT.Exp,
                                             bias=neg_max[:, i % 2, t:t + 1], scale=SC,
                                             accum_out=row_sum[:, (i // 4) % 2, t, i % 4:i % 4 + 1])\
                            .then_inc(sem(f"probs_made{l}"), 1)
                    if kind == "A":
                        nc.scalar.activation(sink_exp[:, (i // 4) % 2, :, i % 4], neg_max[:, i % 2, :],
                                             ACT.Exp, bias=sinks[:, i:i + 1])\
                            .then_inc(sem("sink_made"), 1)

                def second(i, l=l, us=us):
                    PT = PT_t[i % 2]
                    if us[i][0] == "B":
                        j = i - AH
                        act.wait_ge(sem(f"w_made{l}"), j + 1)
                        nc.scalar.activation(PT[:, 0:TRI], PT[:, 0:TRI], ACT.Exp, scale=SC)\
                            .then_inc(sem(f"aT_made{l}"), 1)
                    else:
                        b = wait_filled(act, f"{l}t{i}")
                        if i >= 2:
                            act.wait_ge(sem(f"unit_done{l}"), i - 1)
                        empties(copy(PT[:, 0:TRI], b[:, 0:TRI]), f"{l}t{i}")

                def mem_evacuate(i, l=l):
                    if i >= 4 and i % 4 == 0 and i <= NU:
                        blk = i // 4 - 1
                        name = f"{l}kv{blk}"
                        wait_block(act, name)
                        b = bank_of(f"{name}.0")
                        if blk < 2:
                            if blk == 1:
                                for q in range(2):
                                    wait_filled(act, f"{l}kv0T.{q}")
                            empties(copy(m_stage[:, 0, :], b[:, :]), f"{name}.0")
                        else:
                            empties(copy(MV[:, 0, (blk - 2) * W:(blk - 1) * W], b[:, :]), f"{name}.0")
                    if i in (6, 10):
                        name = f"{l}kv{i // 4 - 1}T"
                        b = wait_filled(act, f"{name}.0")
                        t0 = 4 * (i // 4 - 1)
                        empties(copy(MK[:, t0:t0 + 2, :].rearrange("p k t -> p (k t)"), b[:, :]),
                                f"{name}.0")

                for i in range(NU + 1):
                    if i < NU:
                        first(i)
                    mem_evacuate(i)
                    if i >= 1:
                        second(i - 1)
                    if i % 2 == 1:
                        split(blocks[f"{l}kv0"][0] + i // 2 + NSPL)
                split_to(f"{l}oT", xT_hi)
                last_block(f"{l}out1")
                start_rstd(3 * l)
                split_to(f"{l}n0", xT_hi)
                split(last_chunk(f"{l}out1") + NSPL)

                def mq_evacuate(i, l=l):
                    b = wait_filled(act, f"{l}mq{i}T.0")
                    empties(copy(QK[:, 4 * i:4 * i + 2, :].rearrange("p k t -> p (k t)"), b[:, :]),
                            f"{l}mq{i}T.0")

                for i in range(2):
                    name = f"{l}mq{i}"
                    if i:
                        split(blocks[name][0] + NSPL)
                        mq_evacuate(0)
                    after(name)
                    empties(copy(stage[:, i, 0, :], bank_of(f"{name}.0")[:, :]), f"{name}.0")
                mq_evacuate(1)
                split(last_chunk(f"{l}mq1") + NSPL)
                for h in range(MH + 1):
                    if h < MH:
                        act.wait_ge(sem(f"m_max_made{l}"), h + 1)
                        if h >= 2:
                            wait_filled(act, f"{l}mt{h - 2}")
                        b = bank_of(f"{l}ms{h}")
                        for t in range(TB):
                            ins = nc.scalar.activation(
                                P_t[h % 2][:, t * SEQ:(t + 1) * SEQ], b[:, t * SEQ:(t + 1) * SEQ],
                                ACT.Exp, bias=neg_max[:, h % 2, t:t + 1], scale=MSC,
                                accum_out=row_sum[:, 0, t, h:h + 1])
                            ins.then_inc(sem(f"m_probs_made{l}"), 1)
                        act.wait_ge(sem(f"m_probs_made{l}"), 2 * (h + 1))
                        empties(nc.scalar.nop(), f"{l}ms{h}")
                    if h >= 1:
                        i = h - 1
                        b = wait_filled(act, f"{l}mt{i}")
                        if i >= 2:
                            wait_filled(act, f"{l}mo{i - 2}")
                        empties(copy(PT_t[i % 2][:, :], b[:, :]), f"{l}mt{i}")
                split_to(f"{l}moT", xT_hi)
                last_block(f"{l}mw1")
                if l == 1:
                    act.wait_ge(sem("r_in"), 16)
                    copy(r_hi[:, :, :], r_w[:, :, :]).then_inc(sem("r_hi"), 1)
                start_rstd(3 * l + 1)
                split_to(f"{l}n1", xT_hi)
                split(last_chunk(f"{l}mw1") + NSPL)

                if l == 0:
                    def h_hi(j):
                        for q in range(FB[j][1] // (2 * P)):
                            b = wait_filled(act, f"0h{j}T.{q}")
                            k = 4 * j + 2 * q
                            copy(hT_hi[:, k:k + 2, :].rearrange("p k t -> p (k t)"), b[:, :])\
                                .then_inc(sem("t_hi"), 1)

                    for j, (_, n) in enumerate(FB):
                        split(blocks[f"0g{j}"][0] + NSPL)
                        if j:
                            h_hi(j - 1)
                        after(f"0g{j}")
                        for t in range(TB):
                            if j:
                                wait_emptied(act, f"0u{j - 1}.{t}")
                            nc.scalar.activation(act_g[:, t, 0:n], bank_of(f"0g{j}.{t}")[:, 0:n],
                                                 ACT.Silu).then_inc(
                                                     emptied[fillings[f"0g{j}.{t}"][0]], 1)
                        split(last_chunk(f"0u{j}") + NSPL - 1)
                    split(blocks["0dn0"][0] + NSPL)
                    h_hi(len(FB) - 1)
                    act.wait_ge(sem("f_in"), 16)
                    copy(f_hi[:, :, :], f_w[:, :, :]).then_inc(sem("f_hi"), 1)
                    last_block("0dn1")
                    start_rstd(2)
                    split_to("0n2", xT_hi)
                    split(last_chunk("0dn1") + NSPL)

            act.wait_ge(sem("normed"), 2 * 5)
            for t in range(TB):
                ins = copy(xr_hi[:, t, :], X[:, t, :])
                ins.then_inc(sem("xr_hi_made"), 1)
            act.wait_ge(sem("gap_made"), 1)
            nc.scalar.activation(gap[:, :], gap[:, :], ACT.Exp).then_inc(sem("gap_exp"), 1)

            def gathered(tag, job):
                for half in range(2):
                    b = wait_filled(act, f"{tag}{half}", job)
                    empties(copy(xe_hi[:, 4 * half:4 * half + 4, :].rearrange("p k s -> p (k s)"),
                                 b[:, :]), f"{tag}{half}")

            gathered("gA", None)
            act.wait_ge(sem("rounds_made"), 1)
            n_rounds = act.value_load(rounds[0:1, 0:1], min_val=1, max_val=2)
            assert cursor[0] == N0 + NSPL
            with act.Fori(0, n_rounds * NE) as job:
                for c in range(EC):
                    idx = N0 + c + EC * job

                    def w_split(c=c, idx=idx):
                        s = (N0 + c + NSPL)
                        act.wait_ge(raw_in[s % NRAW], 16 * (s // NRAW + 1 + EC // NRAW * job))
                        act.wait_ge(chunk_used, idx + 1)
                        copy(w_hi[s % NSPL][:, :], raw[s % NRAW][:, :]).then_inc(hi_made, 1)

                    if c < 4 * EJ and c % 4 == 1:
                        j = c // 4
                        act.wait_ge(chunk_used, idx + 1)
                        if j >= 2:
                            act.wait_ge(sem("e_hidden"), EJ * job + j - 1)
                        nc.scalar.activation(e_g[j % 2][:, :], bank_of(f"eg{j}")[:, :], ACT.Silu)\
                            .then_inc(emptied[fillings[f"eg{j}"][0]], 1)
                    if c == 4 * EJ + EK // CK - 1 or c == EC - 1:
                        i = (c - 4 * EJ) // (EK // CK)
                        act.wait_ge(chunk_used, idx + 1)
                        nc.scalar.activation(y_hi[:, i * W:(i + 1) * W], bank_of(f"ed{i}")[:, :],
                                             ACT.Copy, scale=slot_w[:, 0:1]).then_inc(sem("y_hi_made"), 1)
                    if c < EC - NSPL:
                        w_split()
                    else:
                        with act.If(job < n_rounds * NE - 1):
                            w_split()
                        with act.Else():
                            act.nop()
                    if c % 4 == 2 and 1 <= c // 4 <= EJ:
                        j = c // 4 - 1
                        b = wait_filled(act, f"et{j}", job)
                        copy(eT_hi[:, 4 * j:4 * j + 4, :].rearrange("p k s -> p (k s)"), b[:, :])\
                            .then_inc(sem("eT_hi_made"), 1)
                gathered("gB", job)
            start_rstd(5)

        @block.vector
        def _(dve):
            cursor = [0]
            chain = [0]
            t_hi = [0]
            tt = nc.vector.tensor_tensor

            def link(ins):
                chain[0] += 1
                ins.then_inc(sem("dve_chain"), 1)
                dve.wait_ge(sem("dve_chain"), chain[0])

            def copy(dst, src):
                return nc.vector.tensor_copy(dst, src)

            def split(upto):
                while cursor[0] <= min(upto, N0 + NSPL - 1):
                    c = cursor[0]
                    cursor[0] += 1
                    n = CHUNK if c >= N0 else chunks[c][1] * chunks[c][2]
                    dve.wait_ge(hi_made, c + 1)
                    tt(w_lo[c % NSPL][:, 0:n], raw[c % NRAW][:, 0:n],
                       w_hi[c % NSPL][:, 0:n].bitcast(F32), ALU.subtract).then_inc(lo_made, 1)

            def rest(dst, b, hi, key):
                t_hi[0] += 1
                dve.wait_ge(sem("t_hi"), t_hi[0])
                empties(tt(dst, b[:, :], hi.bitcast(F32), ALU.subtract), key)

            def split_to(key, hi, lo):
                for q in range(4):
                    flat = "p k t -> p (k t)"
                    rest(lo[:, 2 * q:2 * q + 2, :].rearrange(flat), bank_of(f"{key}.{q}"),
                         hi[:, 2 * q:2 * q + 2, :].rearrange(flat), f"{key}.{q}")

            def after(name):
                split(last_chunk(name) + NSPL - 1)
                wait_block(dve, name)

            def add_residual(name, half, t):
                key = f"{name}.{t}"
                xs = X[:, t, half * W:(half + 1) * W]
                empties(nc.vector.scalar_tensor_tensor(out=xs, in0=xs, scalar=ALPHA,
                                                       in1=bank_of(key)[:, :], op0=ALU.mult,
                                                       op1=ALU.add), key)
                wait_emptied(dve, key)
                link(nc.vector.bn_stats(stats[:, t, half, :], xs))

            def norm(n, t):
                xt, r, w = X[:, t, :], rstd[:, t:t + 1], newton[:, t:t + 1]
                v = var_eps[:, t:t + 1]
                link(nc.vector.bn_aggr(mean_var[:, t, :],
                                       stats[:, t, :, :].rearrange("p a b -> p (a b)")))
                nc.vector.tensor_scalar(v, mean_var[:, t, 1:2], LN_EPS, None, ALU.add)\
                    .then_inc(sem("var_made"), 1)
                dve.wait_ge(sem("ln_in"), 32 * (n + 1))
                link(nc.vector.scalar_tensor_tensor(out=xt, in0=xt, scalar=mean_var[:, t, 0:1],
                                                    in1=gb[:, 0, :], op0=ALU.subtract, op1=ALU.mult))
                dve.wait_ge(sem("rstd_made"), 2 * n + t + 1)
                link(nc.vector.tensor_scalar(w, r, r, v, ALU.mult, ALU.mult))
                link(nc.vector.tensor_scalar(w, w, -0.5, 1.5, ALU.mult, ALU.add))
                link(tt(r, r, w, ALU.mult))
                nc.vector.scalar_tensor_tensor(out=xt, in0=xt, scalar=r, in1=gb[:, 1, :], op0=ALU.mult,
                                               op1=ALU.add).then_inc(sem("normed"), 1)

            def end_sublayer(names, n):
                after(names[0])
                for t in range(TB):
                    add_residual(names[0], 0, t)
                split(last_chunk(names[1]) + 1)
                for t in range(TB):
                    if t == 0:
                        wait_filled(dve, f"{names[1]}.0")
                    else:
                        wait_block(dve, names[1])
                    add_residual(names[1], 1, t)
                    norm(n, t)

            split_to("0x", xT_hi, xT_lo)
            split(NSPL - 1)
            split_to("m", mT_hi, mT_lo)
            dve.wait_ge(sem("masks0"), 1)
            nc.vector.scalar_tensor_tensor(out=dist[:, :], in0=dist[:, :], scalar=-1.0, in1=dist[:, :],
                                           op0=ALU.mult, op1=ALU.max)\
                .then_inc(sem("dist_abs"), 1)
            dve.wait_ge(sem("sink_in"), 16)
            link(nc.vector.tensor_scalar(neg_sinks[:, :], sinks[:, :], -1.0, None, ALU.mult))

            for l in range(2):
                names = [n for n, *_ in QKV[l]]
                if l == 1:
                    b = wait_filled(dve, "f")
                    dve.wait_ge(sem("b_in"), 16)
                    for t in range(TB):
                        ins = tt(softp[:, t, :], b[:, t * CH:(t + 1) * CH], gate_b[:, :], ALU.add)
                        if t == 0:
                            link(ins)
                    empties(ins, "f")
                    wait_emptied(dve, "f")
                    link(nc.vector.tensor_scalar(softp[:, :, :], softp[:, :, :], -1.0, None, ALU.mult))
                    nc.vector.tensor_scalar(softp_t[:, :, :], softp[:, :, :], 40.0, None, ALU.min)\
                        .then_inc(sem("fu_made"), 1)
                    dve.wait_ge(sem("fl_made"), 1)
                    link(tt(softp[:, :, :], softp[:, :, :], softp_t[:, :, :], ALU.max))
                    nc.vector.tensor_scalar(softp[:, :, :], softp[:, :, :], 1.0 / SC, None, ALU.mult)\
                        .then_inc(sem("softp_made"), 1)

                def qk_evacuate(name, l=l):
                    if name == "akv":
                        return
                    b = wait_filled(dve, f"{l}{name}T.1")
                    t0 = TILES[l][name] + 2
                    empties(copy(QK[:, t0:t0 + 2, :].rearrange("p k t -> p (k t)"), b[:, :]),
                            f"{l}{name}T.1")

                for i, name in enumerate(names):
                    if i and names[i - 1] in TILES[l]:
                        split(blocks[f"{l}{name}"][0] + NSPL - 1)
                        qk_evacuate(names[i - 1])
                    after(f"{l}{name}")
                    key = f"{l}{name}.1"
                    src = bank_of(key)
                    if name in TILES[l]:
                        back = [n for n in names[:i] if n in TILES[l]]
                        if len(back) >= 2:
                            for q in range(1 if back[-2] == "akv" else 2):
                                wait_filled(dve, f"{l}{back[-2]}T.{q}")
                        dst = stage[:, len(back) % 2, 1, :]
                    if name == "akv":
                        kv = dst[:, 0:2 * P].rearrange("p (h r d) -> p h r d", h=KVH, r=2)
                        s = src[:, 0:P].rearrange("p (h d) -> p h d", h=KVH)
                        copy(kv[:, :, 0, :], s)
                        copy(kv[:, :, 1, :], s)
                        empties(copy(V[:, 1, 0:P], src[:, P:2 * P]), key)
                    elif name in TILES[l]:
                        empties(copy(dst, src[:, :]), key)
                    else:
                        v0 = VALUES[l][name]
                        empties(copy(V[:, 1, v0:v0 + W], src[:, :]), key)
                dve.wait_ge(sem(f"masks{l}"), 2 - l)
                us = units(l)

                def first(i, l=l, us=us):
                    kind, h = us[i][0], us[i][5]
                    S, key = S_t[i % 2], f"{l}s{i}"
                    b = wait_filled(dve, key)
                    if kind == "B":
                        if i < AH + 2:
                            dve.wait_ge(sem(f"probs_made{l}"), 2 * (i - 1))
                        nc.vector.tensor_scalar(S[:, 0:TRI], b[:, 0:TRI], SC, 40.0, ALU.mult, ALU.min)\
                            .then_inc(sem(f"zc_made{l}"), 1)
                        return
                    if i >= 2:
                        dve.wait_ge(sem(f"probs_made{l}"), 2 * (i - 1))
                    if kind == "A":
                        slope = 2.0 ** (-8.0 * (h + 1) / AH)
                        empties(nc.vector.scalar_tensor_tensor(
                            out=S[:, 0:TRI], in0=dist[:, :], scalar=-slope / SC, in1=b[:, 0:TRI],
                            op0=ALU.mult, op1=ALU.add), key)
                    else:
                        empties(tt(S[:, 0:TRI], b[:, 0:TRI], c_add[:, :], ALU.add), key)
                    wait_emptied(dve, key)
                    if kind == "A" and i >= 2:
                        dve.wait_ge(sem("sink_made"), i - 1)
                    nc.vector.tensor_reduce(row_max[:, i % 2, 0:1], S[:, 0:P], AX_X, ALU.max)
                    link(nc.vector.tensor_reduce(row_max[:, i % 2, 1:2], S[:, P:TRI], AX_X, ALU.max))
                    if kind == "A":
                        nc.vector.tensor_scalar(neg_max[:, i % 2, :], row_max[:, i % 2, :], -SC,
                                                neg_sinks[:, h:h + 1], ALU.mult, ALU.min)\
                            .then_inc(sem(f"max_made{l}"), 1)
                    else:
                        nc.vector.tensor_scalar(neg_max[:, i % 2, :], row_max[:, i % 2, :], -SC, None,
                                                ALU.mult).then_inc(sem(f"max_made{l}"), 1)

                def first_end(i, l=l, us=us):
                    if us[i][0] != "B":
                        return
                    j, S, key = i - AH, S_t[i % 2], f"{l}s{i}"
                    dve.wait_ge(sem(f"lnz_made{l}"), j + 1)
                    link(nc.vector.scalar_tensor_tensor(out=S[:, 0:TRI], in0=bank_of(key)[:, 0:TRI],
                                                        scalar=SC, in1=S[:, 0:TRI], op0=ALU.mult,
                                                        op1=ALU.max))
                    nc.vector.nop().then_inc(emptied[fillings[key][0]], 1)
                    wait_filled(dve, f"{l}t{i - 2}")
                    tt(P_t[i % 2][:, 0:TRI], S[:, 0:TRI], b_neg8[:, :], ALU.mult)\
                        .then_inc(sem(f"logs_made{l}"), 1)

                def second(i, l=l, us=us):
                    if us[i][0] != "B":
                        return
                    key = f"{l}t{i}"
                    b = wait_filled(dve, key)
                    dve.wait_ge(sem(f"unit_done{l}"), i - 1)
                    link(tt(PT_t[i % 2][:, 0:TRI], b[:, 0:TRI], b_add[:, :], ALU.add))
                    nc.vector.nop().then_inc(emptied[fillings[key][0]], 1)
                    nc.vector.nop().then_inc(sem(f"w_made{l}"), 1)

                def outputs(g, l=l, us=us):
                    dve.wait_ge(sem(f"unit_done{l}"), 4 * g + 4)
                    kind = us[4 * g][0]
                    src = bank[7][:, :].rearrange("p (t u d) -> p t u d", t=TB, u=4)
                    dst = O[:, :, g * 4 * DH:(g + 1) * 4 * DH].rearrange("p t (u d) -> p t u d", u=4)
                    if kind == "B":
                        ins = copy(dst, src)
                    else:
                        rs = row_sum[:, g % 2, :, :]
                        if kind == "A":
                            dve.wait_ge(sem("sink_made"), 4 * g + 4)
                            link(tt(row_inv[:, :, :], rs, sink_exp[:, g % 2, :, :], ALU.add))
                            link(nc.vector.reciprocal(row_inv[:, :, :], row_inv[:, :, :]))
                        else:
                            link(nc.vector.reciprocal(row_inv[:, :, :], rs))
                        inv = row_inv[:, :, :].unsqueeze(3).broadcast_to([P, TB, 4, DH])
                        ins = tt(dst, src, inv, ALU.mult)
                    link(ins)
                    nc.vector.nop().then_inc(emptied[7], 1)
                    nc.vector.nop().then_inc(sem(f"o_made{l}"), 1)

                def mem_evacuate(i, l=l):
                    if i >= 4 and i % 4 == 0 and i <= NU:
                        blk = i // 4 - 1
                        name = f"{l}kv{blk}"
                        wait_block(dve, name)
                        b = bank_of(f"{name}.1")
                        if blk < 2:
                            if blk == 1:
                                for q in range(2):
                                    wait_filled(dve, f"{l}kv0T.{q}")
                            empties(copy(m_stage[:, 1, :], b[:, :]), f"{name}.1")
                        else:
                            empties(copy(MV[:, 1, (blk - 2) * W:(blk - 1) * W], b[:, :]), f"{name}.1")
                    if i in (6, 10):
                        name = f"{l}kv{i // 4 - 1}T"
                        b = wait_filled(dve, f"{name}.1")
                        t0 = 4 * (i // 4 - 1) + 2
                        empties(copy(MK[:, t0:t0 + 2, :].rearrange("p k t -> p (k t)"), b[:, :]),
                                f"{name}.1")

                for i in range(NU + 2):
                    if i < NU:
                        first(i)
                    mem_evacuate(i)
                    if 1 <= i <= NU:
                        second(i - 1)
                    if i < NU:
                        first_end(i)
                    if i >= 2 and (i - 2) % 4 == 3:
                        outputs((i - 2) // 4)
                    if i % 2 == 1 and i < NU:
                        split(blocks[f"{l}kv0"][0] + i // 2 + NSPL)
                split_to(f"{l}oT", xT_hi, xT_lo)
                end_sublayer([f"{l}out0", f"{l}out1"], 3 * l)
                split_to(f"{l}n0", xT_hi, xT_lo)
                split(last_chunk(f"{l}out1") + NSPL)

                def mq_evacuate(i, l=l):
                    b = wait_filled(dve, f"{l}mq{i}T.1")
                    empties(copy(QK[:, 4 * i + 2:4 * i + 4, :].rearrange("p k t -> p (k t)"), b[:, :]),
                            f"{l}mq{i}T.1")

                for i in range(2):
                    name = f"{l}mq{i}"
                    if i:
                        split(blocks[name][0] + NSPL)
                        mq_evacuate(0)
                    after(name)
                    empties(copy(stage[:, i, 1, :], bank_of(f"{name}.1")[:, :]), f"{name}.1")
                mq_evacuate(1)
                split(last_chunk(f"{l}mq1") + NSPL)
                for h in range(MH + 2):
                    if h < MH:
                        b = wait_filled(dve, f"{l}ms{h}")
                        if h >= 2:
                            dve.wait_ge(sem(f"m_probs_made{l}"), 2 * (h - 1))
                        link(nc.vector.tensor_reduce(row_max[:, h % 2, :],
                                                     b[:, :].rearrange("p (t s) -> p t s", t=TB),
                                                     AX_X, ALU.max))
                        nc.vector.tensor_scalar(neg_max[:, h % 2, :], row_max[:, h % 2, :], -MSC, None,
                                                ALU.mult).then_inc(sem(f"m_max_made{l}"), 1)
                    if h >= 2:
                        i = h - 2
                        b = wait_filled(dve, f"{l}mo{i}")
                        link(nc.vector.reciprocal(row_inv[:, :, i], row_sum[:, 0, :, i]))
                        for t in range(TB):
                            ins = nc.vector.tensor_scalar(O[:, t, i * MDH:(i + 1) * MDH],
                                                          b[:, t * MDH:(t + 1) * MDH],
                                                          row_inv[:, t, i:i + 1], None, ALU.mult)
                            if t == 0:
                                link(ins)
                        empties(ins, f"{l}mo{i}")
                split_to(f"{l}moT", xT_hi, xT_lo)
                if l == 1:
                    dve.wait_ge(sem("r_hi"), 1)
                    tt(r_lo[:, :, :], r_w[:, :, :], r_hi[:, :, :].bitcast(F32), ALU.subtract)\
                        .then_inc(sem("r_split"), 1)
                end_sublayer([f"{l}mw0", f"{l}mw1"], 3 * l + 1)
                split_to(f"{l}n1", xT_hi, xT_lo)
                if l == 0:
                    split(last_chunk(f"{l}mw1") + NSPL)

                if l == 0:
                    def h_lo(j):
                        for q in range(FB[j][1] // (2 * P)):
                            k = 4 * j + 2 * q
                            flat = "p k t -> p (k t)"
                            rest(hT_lo[:, k:k + 2, :].rearrange(flat), bank_of(f"0h{j}T.{q}"),
                                 hT_hi[:, k:k + 2, :].rearrange(flat), f"0h{j}T.{q}")

                    for j, (_, n) in enumerate(FB):
                        split(blocks[f"0g{j}"][0] + NSPL)
                        if j:
                            h_lo(j - 1)
                        split(last_chunk(f"0u{j}") + NSPL - 1)
                        wait_block(dve, f"0u{j}")
                        for t in range(TB):
                            wait_emptied(dve, f"0g{j}.{t}")
                            if j >= 2:
                                for q in range(2):
                                    wait_filled(dve, f"0h{j - 2}T.{q}")
                            empties(tt(h_tok[j % 2][:, t, 0:n], bank_of(f"0u{j}.{t}")[:, 0:n],
                                       act_g[:, t, 0:n], ALU.mult), f"0u{j}.{t}")
                    split(blocks["0dn0"][0] + NSPL)
                    h_lo(len(FB) - 1)
                    dve.wait_ge(sem("f_hi"), 1)
                    tt(f_lo[:, :, :], f_w[:, :, :], f_hi[:, :, :].bitcast(F32), ALU.subtract)\
                        .then_inc(sem("f_split"), 1)
                    end_sublayer(["0dn0", "0dn1"], 2)
                    split_to("0n2", xT_hi, xT_lo)
                    split(last_chunk("0dn1") + NSPL)

            dve.wait_ge(sem("slot_made"), 1)
            b = wait_filled(dve, "router")
            link(copy(logit[:, :, :].rearrange("p t e -> p (t e)"), b[:, 0:TB * NE]))
            nc.vector.nop().then_inc(emptied[4], 1)
            nc.vector.max(best[:, 0, :], logit[:, 0, :])
            link(nc.vector.max(best[:, 1, :], logit[:, 1, :]))
            nc.vector.max_index(best_i[:, 0, :], best[:, 0, :], logit[:, 0, :])
            link(nc.vector.max_index(best_i[:, 1, :], best[:, 1, :], logit[:, 1, :]))
            link(nc.vector.tensor_scalar(best_f[:, :, :], best_i[:, :, :], 1.0, None, ALU.add))
            expert = slot_no[:, 0:NE].unsqueeze(1).broadcast_to([P, TB, NE])
            tt(hot1[:, :, :], expert, best_f[:, :, 0:1].broadcast_to([P, TB, NE]), ALU.is_equal)
            link(tt(hot2[:, :, :], expert, best_f[:, :, 1:2].broadcast_to([P, TB, NE]), ALU.is_equal))
            tt(taken[:, :, :], hot1[:, :, :], hot2[:, :, :], ALU.add).then_inc(sem("taken_made"), 1)
            tt(gap[:, :], best[:, :, 1], best[:, :, 0], ALU.subtract).then_inc(sem("gap_made"), 1)
            for t in range(TB):
                dve.wait_ge(sem("xr_hi_made"), t + 1)
                tt(xr_lo[:, t, :], X[:, t, :], xr_hi[:, t, :].bitcast(F32), ALU.subtract)\
                    .then_inc(sem("xr_made"), 1)
            nc.vector.memset(wt[:, :, :], 0.0)
            link(nc.vector.memset(place[:, :, :], 0.0))
            b = wait_filled(dve, "places")
            link(nc.vector.scalar_tensor_tensor(
                out=place[:, :, 0:NE], in0=b[:, 0:2 * NE].rearrange("p (t e) -> p t e", t=TB), scalar=1.0,
                in1=taken[:, :, :], op0=ALU.add, op1=ALU.mult))

            def picks(nxt):
                for t in range(TB):
                    ins = nc.vector.tensor_scalar(pick[:, t, :], slot_no[:, :], place[:, t, nxt], None,
                                                  ALU.is_equal)
                ins.then_inc(sem("picked"), 1)

            picks(slice(0, 1))
            split(N0 + NSPL - 1)
            dve.wait_ge(sem("gap_exp"), 1)
            link(nc.vector.tensor_scalar(g1[:, :], gap[:, :], 1.0, None, ALU.add))
            link(nc.vector.reciprocal(g1[:, :], g1[:, :]))
            link(tt(g2[:, :], g1[:, :], gap[:, :], ALU.mult))
            for t in range(TB):
                link(nc.vector.tensor_scalar(hot2[:, t, :], hot2[:, t, :], g2[:, t:t + 1], None,
                                             ALU.mult))
                link(nc.vector.scalar_tensor_tensor(out=wt[:, t, 0:NE], in0=hot1[:, t, :],
                                                    scalar=g1[:, t:t + 1], in1=hot2[:, t, :],
                                                    op0=ALU.mult, op1=ALU.add))
            copy(wt[:, :, NE:2 * NE], wt[:, :, 0:NE]).then_inc(sem("gates_made"), 1)
            nc.vector.tensor_scalar(place[:, :, NE:2 * NE], place[:, :, 0:NE], -float(P), None, ALU.add)
            link(nc.vector.tensor_reduce(most[:, :], bank_of("places")[:, 2 * NE:3 * NE], AX_X, ALU.max))
            nc.vector.nop().then_inc(emptied[5], 1)
            link(nc.vector.tensor_scalar(most[:, :], most[:, :], float(P), 1.0, ALU.is_gt, ALU.add))
            copy(rounds[:, :], most[:, :]).then_inc(sem("rounds_made"), 1)

            def gathered(tag, job):
                for half in range(2):
                    b = wait_filled(dve, f"{tag}{2 + half}", job)
                    empties(copy(xe_lo[:, 4 * half:4 * half + 4, :].rearrange("p k s -> p (k s)"),
                                 b[:, :]), f"{tag}{2 + half}")

            def slots(tag, job, n):
                b = wait_filled(dve, tag, job)
                copy(pickT[:, :, :].rearrange("p t s -> p (t s)"), b[:, 0:2 * P])
                empties(copy(slot_w[:, :], b[:, 2 * P:2 * P + 1]), tag)

            gathered("gA", None)
            slots("pA", None, 0)
            link(nc.vector.tensor_scalar(X[:, :, :], X[:, :, :], ALPHA, None, ALU.mult))
            n_rounds = dve.value_load(rounds[0:1, 0:1], min_val=1, max_val=2)
            with dve.Fori(0, n_rounds * NE) as job:
                for c in range(EC):
                    idx = N0 + c + EC * job
                    if c < 4 * EJ and c % 4 == 3:
                        j = c // 4
                        dve.wait_ge(chunk_used, idx + 1)
                        wait_emptied(dve, f"eg{j}", job)
                        if j >= 2:
                            wait_filled(dve, f"et{j - 2}", job)
                        ins = tt(e_h[j % 2][:, :], bank_of(f"eu{j}")[:, :], e_g[j % 2][:, :], ALU.mult)
                        ins.then_inc(sem("e_hidden"), 1)
                        dve.wait_ge(sem("e_hidden"), EJ * job + j + 1)
                        nc.vector.nop().then_inc(emptied[fillings[f"eu{j}"][0]], 1)
                    if c == 4 * EJ + EK // CK - 1 or c == EC - 1:
                        i = (c - 4 * EJ) // (EK // CK)
                        dve.wait_ge(sem("y_hi_made"), 2 * job + i + 1)
                        empties(nc.vector.scalar_tensor_tensor(
                            out=y_lo[:, i * W:(i + 1) * W], in0=bank_of(f"ed{i}")[:, :],
                            scalar=slot_w[:, 0:1], in1=y_hi[:, i * W:(i + 1) * W].bitcast(F32),
                            op0=ALU.mult, op1=ALU.subtract), f"ed{i}")

                    def w_split(c=c, idx=idx):
                        s = N0 + c + NSPL
                        dve.wait_ge(hi_made, idx + NSPL + 1)
                        tt(w_lo[s % NSPL][:, :], raw[s % NRAW][:, :], w_hi[s % NSPL][:, :].bitcast(F32),
                           ALU.subtract).then_inc(lo_made, 1)

                    if c < EC - NSPL:
                        w_split()
                    else:
                        with dve.If(job < n_rounds * NE - 1):
                            w_split()
                        with dve.Else():
                            dve.nop()
                    if c % 4 == 2 and 1 <= c // 4 <= EJ:
                        j = c // 4 - 1
                        dve.wait_ge(sem("eT_hi_made"), EJ * job + j + 1)
                        empties(tt(eT_lo[:, 4 * j:4 * j + 4, :].rearrange("p k s -> p (k s)"),
                                   bank_of(f"et{j}")[:, :],
                                   eT_hi[:, 4 * j:4 * j + 4, :].rearrange("p k s -> p (k s)").bitcast(F32),
                                   ALU.subtract), f"et{j}")
                    if c == 4 * EJ:
                        picks(bass.ds(job + 1, 1))
                gathered("gB", job)
                for i in range(2):
                    for t in range(TB):
                        key = f"ec{i}{t}"
                        b = wait_filled(dve, key, job)
                        xs = X[:, t, i * W:(i + 1) * W]
                        empties(tt(xs, xs, b[:, :], ALU.add), key)
                slots("pB", job, 1)
            for t in range(TB):
                for half in range(2):
                    wait_emptied(dve, f"ec{half}{t}", n_rounds * NE - 1)
                    link(nc.vector.bn_stats(stats[:, t, half, :], X[:, t, half * W:(half + 1) * W]))
                norm(5, t)


_INS = ["x", "mem", "ln_g", "ln_b", "mem_wq", "mem_wkv", "mem_wo", "ab_w_in", "ab_sinks", "ab_w_out",
        "c_w_in", "c_b_f", "c_w_out", "ffn_w_gate", "ffn_w_up", "ffn_w_down",
        "moe_router", "moe_w_gate", "moe_w_up", "moe_w_down"]


def kernel(**inputs):
    import numpy as _np
    import concourse.bacc as _bacc
    from concourse import mybir as _mybir
    from concourse.bass_utils import run_bass_kernel_spmd as _run

    nc = _bacc.Bacc("TRN2", target_bir_lowering=False, num_devices=1)
    arrays, args = {}, []
    for name in _INS:
        a = _np.ascontiguousarray(inputs[name])
        arrays[f"in_{name}_dram"] = a
        args.append(nc.dram_tensor(f"in_{name}_dram", a.shape, _mybir.dt.from_np(a.dtype),
                                   kind="ExternalInput").ap())
    shape = inputs["x"].shape
    args.append(nc.dram_tensor("out_0_dram", shape, _mybir.dt.float32, kind="ExternalOutput").ap())
    trunk(nc, *args)
    r = _run(nc, [arrays], core_ids=[0])
    return r.results[0]["out_0_dram"]
```

```python
import concourse.bass as bass
from concourse import mybir
from contextlib import ExitStack

F32 = mybir.dt.float32
F32R = mybir.dt.float32r
I32 = mybir.dt.int32
U32 = mybir.dt.uint32
ALU = mybir.AluOpType
ACT = mybir.ActivationFunctionType
AX_X = mybir.AxisListType.X

P = 128
BIG = 1e30
LN_EPS = 1e-5


def trunk(nc, x, mem, ln_g, ln_b, mem_wq, mem_wkv, mem_wo, ab_w_in, ab_sinks, ab_w_out,
          c_w_in, c_b_f, c_w_out, ffn_w_gate, ffn_w_up, ffn_w_down,
          moe_router, moe_w_gate, moe_w_up, moe_w_down, out):
    _, SEQ, D = x.shape
    DEPTH = ln_g.shape[0]
    TB = SEQ // P
    KT = D // P
    DH = 64
    AH = ab_sinks.shape[1]
    KVH = AH // 4
    BH = D // (2 * DH)
    CH = D // DH
    MH = 4
    MDH = D // MH
    DFF = ffn_w_gate.shape[2]
    NE = moe_router.shape[2]
    DE = moe_w_gate.shape[3]
    W = 512
    ALPHA = (2.0 * DEPTH) ** 0.25
    assert (SEQ, D, TB, KT, NE, MEM_LEN := mem.shape[1]) == (256, 1024, 2, 8, 8, 256)
    SC = DH ** -0.5
    MSC = MDH ** -0.5
    TRI = 3 * P

    CK = 4
    chunks = []
    blocks = {}

    def add_block(name, w, col, cols, ck=CK):
        rows = w.shape[0] // P
        sizes = [min(ck, rows - k) for k in range(0, rows, ck)]
        blocks[name] = (len(chunks), sizes, cols)
        k = 0
        for n in sizes:
            src = w[k * P:(k + n) * P, col:col + cols].rearrange("(k p) c -> p k c", p=P)
            chunks.append((src, n, cols))
            k += n

    FB = [(j * W, min(W, DFF - j * W)) for j in range((DFF + W - 1) // W)]
    AQ, BQ = AH * DH, AH * DH + 2 * KVH * DH
    QKV = [[("q0", 0, W, CK), ("akv", AQ, 2 * KVH * DH, 8), ("bq", BQ, W, CK), ("bk", BQ + W, W, CK),
            ("bv", BQ + 2 * W, W, CK)],
           [("q0", 0, W, CK), ("q1", W, W, CK), ("k0", 2 * W, W, CK), ("k1", 3 * W, W, CK),
            ("v0", 4 * W, W, CK), ("v1", 5 * W, W, CK)]]
    for l in range(2):
        w_in = ab_w_in[0] if l == 0 else c_w_in[0]
        for name, col, cols, ck in QKV[l]:
            add_block(f"{l}{name}", w_in, col, cols, ck)
        for i in range(3 - l):
            add_block(f"{l}kv{i}", mem_wkv[l], i * W, W)
        for i in range(2):
            add_block(f"{l}out{i}", ab_w_out[0] if l == 0 else c_w_out[0], i * W, W)
        add_block(f"{l}kv3", mem_wkv[l], 3 * W, W)
        for i in range(2):
            add_block(f"{l}mq{i}", mem_wq[l], i * W, W)
        for i in range(2):
            add_block(f"{l}mw{i}", mem_wo[l], i * W, W)
        if l == 0:
            for j, (c, n) in enumerate(FB):
                add_block(f"0g{j}", ffn_w_gate[0], c, n)
                add_block(f"0u{j}", ffn_w_up[0], c, n)
            for i in range(2):
                add_block(f"0dn{i}", ffn_w_down[0], i * W, W)
            add_block("1kv2", mem_wkv[1], 2 * W, W)
    N0 = len(chunks)
    EJ = DE // W
    EK = DE // P
    EC = 2 * 2 * EJ + 2 * (EK // CK)
    NRAW, NSPL = 6, 3
    NEXP = NRAW + 1
    assert EC % NEXP == 0 and EC % NSPL == 0
    CHUNK = CK * W

    with ExitStack() as ctx:
        arena_bytes = 207 * 1024 + 640
        ctx.enter_context(nc.sbuf_tensor("arena", [P, arena_bytes // 4], F32))
        START = ((nc.sbuf_base - arena_bytes) + 31) // 32 * 32
        top = [START]

        def at(name, shape, dt, off):
            size = 4
            for s in shape[1:]:
                size *= s
            assert off % 32 == 0 and off + size <= START + arena_bytes, (name, off, size)
            return nc.alloc_sbuf_tensor_at(name, shape, dt, offset=off)

        def take(name, shape, dt=F32):
            size = 4
            for s in shape[1:]:
                size *= s
            off = top[0]
            top[0] += (size + 31) // 32 * 32
            return at(name, shape, dt, off)

        raw = [take(f"raw{i}", [P, CHUNK]) for i in range(NRAW)]
        w_hi = [take(f"w_hi{i}", [P, CHUNK], F32R) for i in range(NSPL)]
        w_lo = [take(f"w_lo{i}", [P, CHUNK], F32R) for i in range(NSPL)]
        X = take("X", [P, TB, D])
        o_xt = top[0]
        xT_hi = take("xT_hi", [P, KT, SEQ], F32R)
        xT_lo = take("xT_lo", [P, KT, SEQ], F32R)
        o_mt = top[0]
        mT_hi = take("mT_hi", [P, KT, SEQ], F32R)
        mT_lo = take("mT_lo", [P, KT, SEQ], F32R)
        o_v = top[0]
        V = take("V", [P, TB, D])
        o_region = top[0]
        QK = take("QK", [P, 16, SEQ])
        o_mk = top[0]
        MK = take("MK", [P, KT, SEQ])
        MV = take("MV", [P, TB, D])
        o_o = top[0]
        O = take("O", [P, TB, D])
        o_mask = top[0]
        take("mask_room", [P, 5 * 256])
        o_scr = top[0]
        scratch = take("scratch", [P, 6 * W])
        ident = take("ident", [P, P])
        ones = take("ones", [P, P])
        tri_ge = take("tri_ge", [P, P])
        tri_lt = take("tri_lt", [P, P])
        stats = take("stats", [P, TB, 2, 6])
        mean_var = take("mean_var", [P, TB, 2])
        rstd = take("rstd", [P, TB])
        var_eps = take("var_eps", [P, TB])
        newton = take("newton", [P, TB])
        warm = take("warm", [P, 16])
        row_max = take("row_max", [P, 2, TB])
        neg_max = take("neg_max", [P, 2, TB])
        row_sum = take("row_sum", [P, 2, TB, 4])
        sink_exp = take("sink_exp", [P, 2, TB, 4])
        row_inv = take("row_inv", [P, TB, 4])
        sinks = take("sinks", [P, AH])
        neg_sinks = take("neg_sinks", [P, AH])
        gate_b = take("gate_b", [P, CH])
        f_w = take("f_w", [P, KT, CH])
        f_hi = take("f_hi", [P, KT, CH], F32R)
        f_lo = take("f_lo", [P, KT, CH], F32R)
        softp = take("softp", [P, TB, CH])
        softp_t = take("softp_t", [P, TB, CH])
        mem_tok = at("mem_tok", [P, TB, D], F32, o_mk)
        stage = at("stage", [P, 2, TB, W], F32, o_o)
        m_stage = at("m_stage", [P, TB, W], F32, o_xt)
        gb = at("gb", [P, 2, D], F32, o_v)
        dist = at("dist", [P, TRI], F32, o_mask)
        b_add = at("b_add", [P, TRI], F32, o_mask + 4 * TRI)
        b_neg8 = at("b_neg8", [P, TRI], F32, o_mask + 8 * TRI)
        c_add = at("c_add", [P, TRI], F32, o_mask)
        tri_le = at("tri_le", [P, TRI], F32, o_mask + 4 * TRI)
        f_col = at("f_col", [P, 2, TB, P], F32, o_mask + 8 * TRI)
        S_t = [at(f"S{i}", [P, W], F32, o_scr + 4 * W * i) for i in range(2)]
        P_t = [at(f"P{i}", [P, W], F32, o_scr + 4 * W * (2 + i)) for i in range(2)]
        PT_t = [at(f"PT{i}", [P, W], F32, o_scr + 4 * W * (4 + i)) for i in range(2)]
        FK = DFF // P
        hT_hi = at("hT_hi", [P, FK, SEQ], F32R, o_region)
        hT_lo = at("hT_lo", [P, FK, SEQ], F32R, o_region + 4 * FK * SEQ)
        act_g = at("act_g", [P, TB, W], F32, o_scr)
        h_tok = [at(f"h_tok{i}", [P, TB, W], F32, o_scr + 4 * TB * W * (1 + i)) for i in range(2)]
        eT_hi = at("eT_hi", [P, EK, P], F32R, o_region)
        eT_lo = at("eT_lo", [P, EK, P], F32R, o_region + 4 * EK * P)
        o = o_region + 8 * EK * P
        y_hi = at("y_hi", [P, D], F32R, o)
        y_lo = at("y_lo", [P, D], F32R, o + 4 * D)
        e_g = [at(f"e_g{i}", [P, W], F32, o + 8 * D + 4 * W * i) for i in range(2)]
        xr_hi = at("xr_hi", [P, TB, D], F32R, o_mt)
        xr_lo = at("xr_lo", [P, TB, D], F32R, o_mt + 4 * TB * D)
        raw_exp = [raw[(N0 + i) % NRAW] for i in range(NRAW)]
        raw_exp.append(at("raw_more", [P, CHUNK], F32, o_xt + 8 * KT * P))
        xe_hi = at("xe_hi", [P, KT, P], F32R, o_xt)
        xe_lo = at("xe_lo", [P, KT, P], F32R, o_xt + 4 * KT * P)
        e_h = [at(f"e_h{i}", [P, W], F32, o_scr + 4 * W * i) for i in range(2)]
        pick = at("pick", [P, TB, P], F32R, o_scr + 8 * W)
        pickT = at("pickT", [P, TB, P], F32R, o_scr + 8 * W + 4 * TB * P)
        o = o_scr + 8 * W + 8 * TB * P
        slot_no = at("slot_no", [P, P], F32, o)
        o += 4 * P
        r_w = at("r_w", [P, KT, NE], F32, o)
        r_hi = at("r_hi", [P, KT, NE], F32R, o + 256)
        r_lo = at("r_lo", [P, KT, NE], F32R, o + 512)
        o += 768
        small = {}
        for name, shape, dt in (
                ("logit", [P, TB, NE], F32), ("best", [P, TB, 8], F32), ("best_i", [P, TB, 8], U32),
                ("best_f", [P, TB, 8], F32), ("hot1", [P, TB, NE], F32), ("hot2", [P, TB, NE], F32),
                ("gap", [P, TB], F32), ("g1", [P, TB], F32), ("g2", [P, TB], F32),
                ("taken", [P, TB, NE], F32), ("wt", [P, TB, 3 * NE], F32),
                ("place", [P, TB, 3 * NE], F32), ("most", [P, 1], F32), ("rounds", [P, 1], I32),
                ("slot_w", [P, 1], F32)):
            small[name] = at(name, shape, dt, o)
            size = 4
            for s in shape[1:]:
                size *= s
            o += (size + 31) // 32 * 32
        assert o <= o_scr + 4 * 6 * W, o - o_scr
        logit, best, best_i, best_f = (small[n] for n in ("logit", "best", "best_i", "best_f"))
        hot1, hot2, gap, g1, g2 = (small[n] for n in ("hot1", "hot2", "gap", "g1", "g2"))
        taken, wt, place, most, rounds, slot_w = (
            small[n] for n in ("taken", "wt", "place", "most", "rounds", "slot_w"))

        bank = [ctx.enter_context(nc.psum_tensor(f"bank{i}", [P, W], F32)) for i in range(8)]

        sems = {}

        def sem(name):
            if name not in sems:
                sems[name] = ctx.enter_context(nc.semaphore(name))
            return sems[name]

        raw_in = [sem(f"raw_in{i}") for i in range(NRAW)]
        exp_in = [raw_in[(N0 + i) % NRAW] for i in range(NRAW)] + [sem("raw_more_in")]
        exp_before = [len(range((N0 + i) % NRAW, N0, NRAW)) for i in range(NRAW)] + [0]
        hi_made = sem("hi_made")
        lo_made = sem("lo_made")
        chunk_used = sem("chunk_used")
        filled = [sem(f"filled{i}") for i in range(8)]
        emptied = [sem(f"emptied{i}") for i in range(8)]

        fillings = {}
        claims = [0] * 8
        signals = [0] * 8
        JOB_CLAIMS = [5, 5, 5, 4, 2, 2, 5, 4]
        JOB_SIGNALS = [1, 2, 1, 1, 1, 1, 5, 4]

        def claim(eng, key, b, job=None, signal=True, wait=True):
            if claims[b] and wait:
                eng.wait_ge(emptied[b], claims[b] + (0 if job is None else JOB_CLAIMS[b] * job))
            claims[b] += 1
            signals[b] += signal
            fillings[key] = (b, claims[b], signals[b])
            return bank[b]

        def wait_filled(eng, key, job=None):
            b, _, n = fillings[key]
            eng.wait_ge(filled[b], n + (0 if job is None else JOB_SIGNALS[b] * job))
            return bank[b]

        def wait_emptied(eng, key, job=None):
            b, n, _ = fillings[key]
            eng.wait_ge(emptied[b], n + (0 if job is None else JOB_CLAIMS[b] * job))

        def bank_of(key):
            return bank[fillings[key][0]]

        def empties(ins, key):
            ins.then_inc(emptied[fillings[key][0]], 1)

        def last_chunk(name):
            return blocks[name][0] + len(blocks[name][1]) - 1

        def wait_block(eng, name):
            eng.wait_ge(chunk_used, last_chunk(name) + 1)

        block = ctx.enter_context(nc.Block())

        def units(l):
            if l == 1:
                return [("C", h // 2, 8 + h // 2, 64 * (h % 2), h * DH, h) for h in range(CH)]
            a = [("A", h // 2, 4 + h // 4, 64 * (h % 2), (h // 4) * DH, h) for h in range(AH)]
            b = [("B", 6 + h // 2, 10 + h // 2, 64 * (h % 2), P + h * DH, h) for h in range(BH)]
            return a + b

        NU = 16
        KV_STEPS = [[(0, 2, 4, 6), (8, 9, 10, 11), (12, 13, 14, 15)], [(0, 2, 4, 6), (8, 10, 12, 13)]]
        KV_HALF = [{s: (blk, i) for blk, ss in enumerate(st) for i, s in enumerate(ss)}
                   for st in KV_STEPS]
        KV_DONE = [{ss[-1] + 1: blk for blk, ss in enumerate(st)} for st in KV_STEPS]
        KT_STEP = [{ss[-1] + 2: blk for blk, ss in enumerate(st[:2])} for st in KV_STEPS]
        KT_DONE = [{ss[-1] + 3: blk for blk, ss in enumerate(st[:2])} for st in KV_STEPS]
        KV_SPLIT = [{0: 2} | {s: 3 + n for n, s in enumerate(
            s for ss in st for s in ss[1::2])} for st in KV_STEPS]
        POOL_SPLIT = [{blocks[f"{l}kv0"][0] + n for n in KV_SPLIT[l].values()} for l in range(2)]
        BEHIND = [blocks[name][0] + 2 for name in ("0out1", "0mw1")]\
            + [blocks["0dn1"][0] + len(blocks["0dn1"][1])]\
            + [blocks[name][0] + 2 for name in ("1out1", "1mw1")]
        BY_POOL = set(BEHIND) | POOL_SPLIT[0] | POOL_SPLIT[1]
        TILES = [{"q0": 0, "akv": 4, "bq": 6, "bk": 10}, {"q0": 0, "q1": 4, "k0": 8, "k1": 12}]
        VALUES = [{"bv": P}, {"v0": 0, "v1": W}]
        NORMED = 2 * TB
        LNS = [(l, i) for l in range(2) for i in range(3)]

        @block.tensor
        def _(pe):
            pair = [0]

            def chunk_product(c, outs, lhs_hi, lhs_lo, k0, first, last, cols, idx=None, slot=None,
                              rows=None, done=None, ready=None):
                n = chunks[c][1] if idx is None else CK
                pe.wait_ge(lo_made, c + 1 if idx is None else idx + 1)
                s = c % NSPL if slot is None else slot
                hi = w_hi[s][:, 0:n * cols].rearrange("p (k c) -> p k c", k=n)
                lo = w_lo[s][:, 0:n * cols].rearrange("p (k c) -> p k c", k=n)
                for k in rows or range(n):
                    if ready and (k0 + k) % 2 == 0:
                        wait_emptied(pe, f"{ready}.{(k0 + k) // 2}")
                    for t, dst in outs:
                        xh = lhs_hi[:, k0 + k, t * P:(t + 1) * P]
                        xl = lhs_lo[:, k0 + k, t * P:(t + 1) * P]
                        d = dst[:, 0:cols]
                        nc.tensor.matmul(d, xh, hi[:, k, :], start=(first and k == 0), stop=False)
                        nc.tensor.matmul(d, xh, lo[:, k, :], start=False, stop=False)
                        m = nc.tensor.matmul(d, xl, hi[:, k, :], start=False,
                                             stop=(last and k == n - 1))
                if done is not None:
                    m.then_inc(done, 1)

            def product(name, lhs_hi, lhs_lo, between=None, ready=None, split_end=False):
                c0, sizes, cols = blocks[name]
                p = pair[0] % 2
                pair[0] += 1
                outs = [(t, claim(pe, f"{name}.{t}", 2 * p + t, signal=(split_end and t == 0)))
                        for t in range(TB)]
                k0 = 0
                last = len(sizes) - 1
                for i, n in enumerate(sizes):
                    if split_end and i == last - 1:
                        for t in range(TB):
                            for j in (i, i + 1):
                                chunk_product(c0 + j, outs[t:t + 1], lhs_hi, lhs_lo,
                                              k0 + (j - i) * n, j == 0, j == last, cols, ready=ready,
                                              done=chunk_used if t else filled[2 * p] if j == last
                                              else None)
                        break
                    chunk_product(c0 + i, outs, lhs_hi, lhs_lo, k0, i == 0, i == last, cols,
                                  done=chunk_used, ready=ready)
                    k0 += n
                    if between is not None:
                        between(i)

            def transposes(key, src, tiles, b0, ready=None):
                dst = [claim(pe, f"{key}.{q // 2}", b0 + q // 2) for q in range(0, tiles, 2)]
                for t in range(TB):
                    for k in range(tiles):
                        if ready is not None and k % (tiles // 2) == 0:
                            name, n = ready[t]
                            pe.wait_ge(name, n if k else n - 1)
                        c = (k % 2) * SEQ + t * P
                        m = nc.tensor.transpose(dst[k // 2][:, c:c + P], src[:, t, k * P:(k + 1) * P],
                                                ident[:, :])
                        if t == TB - 1 and (k % 2 or k == tiles - 1):
                            m.then_inc(filled[b0 + k // 2], 1)

            def narrow(name, w_h, w_l, n, ready, staged, sb):
                dst = claim(pe, f"{name}0", 4)
                for k in range(KT):
                    if k % 2 == 0:
                        wait_emptied(pe, f"{ready}.{k // 2}")
                    d = dst[0:n, 0:SEQ]
                    nc.tensor.matmul(d, w_h[:, k, :], xT_hi[:, k, :], start=(k == 0), stop=False)
                    nc.tensor.matmul(d, w_l[:, k, :], xT_hi[:, k, :], start=False, stop=False)
                    m = nc.tensor.matmul(d, w_h[:, k, :], xT_lo[:, k, :], start=False,
                                         stop=(k == KT - 1))
                m.then_inc(filled[4], 1)
                pe.wait_ge(sem(staged), 1)
                dst = claim(pe, name, 5)
                for t in range(TB):
                    m = nc.tensor.transpose(dst[:, t * n:(t + 1) * n], sb[0:n, t * P:(t + 1) * P],
                                            ident[0:n, 0:n])
                m.then_inc(filled[5], 1)

            pe.wait_ge(sem("ident_made"), 1)
            pe.wait_ge(sem("x_in"), 16)
            transposes("0x", X, KT, 0)

            def mem_transposes(c):
                if c == 0:
                    pe.wait_ge(sem("mem_in"), 16)
                    transposes("m", mem_tok, KT, 4)

            ready = "0x"

            for l in range(2):
                names = [n for n, *_ in QKV[l]]
                tjob = [0]
                if l == 1:
                    pe.wait_ge(sem("f_split"), 1)
                    narrow("f", f_hi, f_lo, CH, ready, "f_T_made", P_t[0])

                def qk_transposes(name, l=l, tjob=tjob):
                    for t in range(TB):
                        wait_emptied(pe, f"{l}{name}.{t}")
                    tiles = 2 if name == "akv" else 4
                    transposes(f"{l}{name}T", stage[:, tjob[0] % 2, :, :], tiles, 4 + 2 * (tjob[0] % 2))
                    tjob[0] += 1

                for i, name in enumerate(names):
                    before = names[i - 1] if i and names[i - 1] in TILES[l] else None
                    product(f"{l}{name}", xT_hi, xT_lo, ready=ready,
                            between=mem_transposes if l == 0 and i == 0 else
                            (lambda c, b=before: qk_transposes(b) if c == 0 and b else None))
                    if l == 0 and i == 1:
                        pe.wait_ge(sem("consts"), 1)
                for name in names:
                    if name in TILES[l]:
                        for q in range(1 if name == "akv" else 2):
                            wait_emptied(pe, f"{l}{name}T.{q}")

                us = units(l)

                def scores(i, l=l, us=us):
                    kind, q, k, base, _, h = us[i]
                    b = 4 + i % 3
                    d = claim(pe, f"{l}s{i}", b)
                    rows = slice(base, base + DH)
                    qT, kT = QK[rows, q, :], QK[rows, k, :]
                    if kind == "B":
                        nc.tensor.matmul(d[:, 0:SEQ], kT[:, 0:P], qT, start=True, stop=False,
                                         skip_group_check=True)
                        m = nc.tensor.matmul(d[:, SEQ:TRI], kT[:, P:SEQ], qT[:, P:SEQ], start=False,
                                             stop=True, skip_group_check=True)
                    else:
                        c = kind == "C"
                        if c:
                            pe.wait_ge(sem("f_col_made"), i + 1)
                            nc.tensor.matmul(d[:, 0:TRI], f_col[:, i % 2, 0, :], tri_le[:, :],
                                             start=True, stop=False, skip_group_check=True)
                            nc.tensor.matmul(d[:, SEQ:TRI], f_col[:, i % 2, 1, :], tri_le[:, 0:P],
                                             start=False, stop=False, skip_group_check=True)
                        nc.tensor.matmul(d[:, 0:P], qT[:, 0:P], kT[:, 0:P], start=not c, stop=True,
                                         skip_group_check=True)
                        m = nc.tensor.matmul(d[:, P:TRI], qT[:, P:SEQ], kT, start=not c, stop=True,
                                             skip_group_check=True)
                    m.then_inc(filled[b], 1)

                def second(i, l=l, us=us):
                    kind = us[i][0]
                    b = 4 + i % 3
                    src = P_t[i % 2]
                    if kind == "B":
                        pe.wait_ge(sem(f"logs_made{l}"), i + 1 - AH)
                        d = claim(pe, f"{l}t{i}", b)
                        nc.tensor.matmul(d[:, 0:SEQ], tri_ge[:, :], src[:, 0:SEQ], start=False,
                                         stop=False, skip_group_check=True)
                        nc.tensor.matmul(d[:, P:SEQ], ones[:, :], src[:, SEQ:TRI], start=False,
                                         stop=False, skip_group_check=True)
                        m = nc.tensor.matmul(d[:, SEQ:TRI], tri_ge[:, :], src[:, SEQ:TRI],
                                             start=False, stop=True, skip_group_check=True)
                    else:
                        pe.wait_ge(sem(f"probs_made{l}"), 2 * (i + 1))
                        d = claim(pe, f"{l}t{i}", b)
                        for q in range(3):
                            m = nc.tensor.transpose(d[:, q * P:(q + 1) * P], src[:, q * P:(q + 1) * P],
                                                    ident[:, :])
                    m.then_inc(filled[b], 1)

                def values(i, l=l, us=us):
                    kind, vcol = us[i][0], us[i][4]
                    if kind == "B":
                        pe.wait_ge(sem(f"aT_made{l}"), i + 1 - AH)
                    else:
                        wait_emptied(pe, f"{l}t{i}")
                    if i == 0:
                        for name in names:
                            for t in range(TB if name not in TILES[l] else 0):
                                wait_emptied(pe, f"{l}{name}.{t}")
                    if i % 4 == 0:
                        claim(pe, f"{l}o{i // 4}", 7, signal=False)
                    pT = PT_t[i % 2]
                    d = bank[7][:, :].rearrange("p (t u d) -> p t u d", t=TB, u=4)[:, :, i % 4, :]
                    nc.tensor.matmul(d[:, 0, :], pT[:, 0:P], V[:, 0, vcol:vcol + DH], start=True,
                                     stop=True, skip_group_check=True)
                    nc.tensor.matmul(d[:, 1, :], pT[:, P:SEQ], V[:, 0, vcol:vcol + DH], start=True,
                                     stop=False, skip_group_check=True)
                    nc.tensor.matmul(d[:, 1, :], pT[:, SEQ:TRI], V[:, 1, vcol:vcol + DH], start=False,
                                     stop=True, skip_group_check=True).then_inc(sem(f"unit_done{l}"), 1)

                fill_outs = [None]

                def mem_kv(i, l=l, fill_outs=fill_outs):
                    if i not in KV_HALF[l]:
                        return
                    blk, half = KV_HALF[l][i]
                    name = f"{l}kv{blk}"
                    if half == 0:
                        p = pair[0] % 2
                        pair[0] += 1
                        fill_outs[0] = [(t, claim(pe, f"{name}.{t}", 2 * p + t, signal=False))
                                        for t in range(TB)]
                    c = half // 2
                    chunk_product(blocks[name][0] + c, fill_outs[0], mT_hi, mT_lo, 4 * c,
                                  c == 0, c == 1, W, rows=((0, 1), (2, 3))[half % 2],
                                  done=chunk_used if half % 2 else None, ready="m")

                def mem_kT(i, l=l):
                    if i not in KT_STEP[l]:
                        return
                    name = f"{l}kv{KT_STEP[l][i]}"
                    for t in range(TB):
                        wait_emptied(pe, f"{name}.{t}")
                    transposes(f"{name}T", m_stage, 4, 2 * (pair[0] % 2))
                    pair[0] += 1

                for i in range(NU + 2):
                    if i < NU:
                        scores(i)
                    mem_kT(i)
                    mem_kv(i)
                    if 1 <= i <= NU:
                        second(i - 1)
                    if i >= 2:
                        values(i - 2)

                def normed_T(key, n):
                    transposes(key, X, KT, 4, ready=[(sem("normed"), NORMED * n + 2 * (t + 1))
                                                     for t in range(TB)])

                def normed_T_beside(key, n, name):
                    p = pair[0] % 2
                    pair[0] += 1
                    outs = [(t, claim(pe, f"{name}.{t}", 2 * p + t, signal=False)) for t in range(TB)]
                    chunk_product(blocks[name][0], outs, mT_hi, mT_lo, 0, True, False, W,
                                  done=chunk_used)
                    normed_T(key, n)
                    chunk_product(blocks[name][0] + 1, outs, mT_hi, mT_lo, CK, False, True, W,
                                  done=chunk_used)

                transposes(f"{l}oT", O, KT, 4, ready=[(sem(f"o_made{l}"), NU // 4)] * TB)
                for i in range(2):
                    product(f"{l}out{i}", xT_hi, xT_lo, ready=f"{l}oT", split_end=(i == 1))
                normed_T_beside(f"{l}n0", 3 * l, f"{l}kv3")

                stage_m = [f"{l}mq0", f"{l}mq1"]

                def mq_transposes(i, l=l):
                    for t in range(TB):
                        wait_emptied(pe, f"{l}mq{i}.{t}")
                    transposes(f"{l}mq{i}T", stage[:, i, :, :], 4, 4 + 2 * i)

                product(stage_m[0], xT_hi, xT_lo, ready=f"{l}n0")
                product(stage_m[1], xT_hi, xT_lo, between=lambda c: mq_transposes(0) if c == 0 else None)
                mq_transposes(1)
                for q in range(2):
                    for name in stage_m:
                        wait_emptied(pe, f"{name}T.{q}")
                for h in range(MH + 2):
                    if h < MH:
                        b = 4 + h % 3
                        d = claim(pe, f"{l}ms{h}", b)
                        for t in range(TB):
                            for k in range(2):
                                m = nc.tensor.matmul(d[:, t * SEQ:(t + 1) * SEQ],
                                                     QK[:, 2 * h + k, t * P:(t + 1) * P],
                                                     MK[:, 2 * h + k, :], start=(k == 0), stop=(k == 1))
                        m.then_inc(filled[b], 1)
                    if 1 <= h <= MH:
                        i, b = h - 1, 4 + (h - 1) % 3
                        pe.wait_ge(sem(f"m_probs_made{l}"), 2 * (i + 1))
                        d = claim(pe, f"{l}mt{i}", b)
                        for mb in range(2):
                            for t in range(TB):
                                m = nc.tensor.transpose(
                                    d[:, mb * SEQ + t * P:mb * SEQ + (t + 1) * P],
                                    P_t[i % 2][:, t * SEQ + mb * P:t * SEQ + (mb + 1) * P], ident[:, :])
                        m.then_inc(filled[b], 1)
                    if h >= 2:
                        i = h - 2
                        b = 2 + i % 2
                        wait_emptied(pe, f"{l}mt{i}")
                        d = claim(pe, f"{l}mo{i}", b)
                        for t in range(TB):
                            for mb in range(2):
                                m = nc.tensor.matmul(
                                    d[:, t * MDH:(t + 1) * MDH],
                                    PT_t[i % 2][:, mb * SEQ + t * P:mb * SEQ + (t + 1) * P],
                                    MV[:, mb, i * MDH:(i + 1) * MDH], start=(mb == 0), stop=(mb == 1))
                        m.then_inc(filled[b], 1)
                for i in range(MH):
                    wait_emptied(pe, f"{l}mo{i}")
                transposes(f"{l}moT", O, KT, 4)
                for i in range(2):
                    product(f"{l}mw{i}", xT_hi, xT_lo, ready=f"{l}moT", split_end=(i == 1))
                normed_T(f"{l}n1", 3 * l + 1)
                ready = f"{l}n1"

                if l == 0:
                    def h_transposes(j):
                        for t in range(TB):
                            wait_emptied(pe, f"0u{j}.{t}")
                        transposes(f"0h{j}T", h_tok[j % 2], FB[j][1] // P, 4 + 2 * (j % 2))

                    for j in range(len(FB)):
                        product(f"0g{j}", xT_hi, xT_lo, ready=ready,
                                between=(lambda c, j=j: h_transposes(j - 1) if c == 0 and j else None))
                        product(f"0u{j}", xT_hi, xT_lo)

                    def down_between(i, c):
                        if i == 0 and c == 0:
                            h_transposes(len(FB) - 1)
                        if i == 0 and c == 3:
                            for j in range(len(FB)):
                                for q in range(FB[j][1] // (2 * P)):
                                    wait_emptied(pe, f"0h{j}T.{q}")

                    for j in range(len(FB) - 1):
                        for q in range(2):
                            if j < len(FB) - 2:
                                wait_emptied(pe, f"0h{j}T.{q}")
                    for i in range(2):
                        product(f"0dn{i}", hT_hi, hT_lo, between=lambda c, i=i: down_between(i, c),
                                split_end=(i == 1))
                    normed_T_beside("0n2", 2, "1kv2")
                    ready = "0n2"

            pe.wait_ge(sem("r_split"), 1)
            narrow("router", r_hi, r_lo, NE, ready, "r_T_made", e_h[0])
            pe.wait_ge(sem("taken_made"), 1)
            d = claim(pe, "places", 4)
            nc.tensor.matmul(d[:, 0:NE], tri_lt[:, :], taken[:, 0, :], start=True, stop=True,
                             skip_group_check=True)
            nc.tensor.matmul(d[:, NE:2 * NE], ones[:, :], taken[:, 0, :], start=True, stop=False,
                             skip_group_check=True)
            nc.tensor.matmul(d[:, NE:2 * NE], tri_lt[:, :], taken[:, 1, :], start=False, stop=True,
                             skip_group_check=True)
            for t in range(TB):
                m = nc.tensor.matmul(d[:, 2 * NE:3 * NE], ones[:, :], taken[:, t, :], start=(t == 0),
                                     stop=(t == 1), skip_group_check=True)
            m.then_inc(filled[4], 1)

            def gather(tag, job):
                for half in range(2):
                    for part, src in enumerate((xr_hi, xr_lo)):
                        b = 2 * part + half
                        d = claim(pe, f"{tag}{b}", b, job)
                        for kk in range(4):
                            k = 4 * half + kk
                            for t in range(TB):
                                m = nc.tensor.matmul(d[:, kk * P:(kk + 1) * P],
                                                     src[:, t, k * P:(k + 1) * P], pick[:, t, :],
                                                     start=(t == 0), stop=(t == 1))
                        m.then_inc(filled[b], 1)

            def slots(tag, job, nxt):
                d = claim(pe, tag, 1, job)
                for t in range(TB):
                    nc.tensor.transpose(d[:, t * P:(t + 1) * P], pick[:, t, :].bitcast(F32), ident[:, :])
                for t in range(TB):
                    m = nc.tensor.matmul(d[:, 2 * P:2 * P + 1], pick[:, t, :].bitcast(F32),
                                         wt[:, t, nxt], start=(t == 0), stop=(t == 1),
                                         skip_group_check=True)
                m.then_inc(filled[1], 1)

            pe.wait_ge(sem("xr_made"), 2)
            pe.wait_ge(sem("picked"), 1)
            gather("gA", None)
            pe.wait_ge(sem("gates_made"), 1)
            slots("pA", None, slice(0, 1))
            pe.wait_ge(sem("rounds_made"), 1)
            n_rounds = pe.value_load(rounds[0:1, 0:1], min_val=1, max_val=2)
            before = [list(claims), list(signals)]
            with pe.Fori(0, n_rounds * NE) as job:
                start = list(claims)
                for c in range(EC):
                    idx = N0 + c + EC * job
                    if c < 2:
                        for b in (c, 2 + c):
                            pe.wait_ge(emptied[b], start[b] - (1 if b == 1 else 0)
                                       + JOB_CLAIMS[b] * job)
                    if c < 4 * EJ:
                        j, q = c // 4, c % 4
                        key, b = (f"eg{j}", j % 2) if q < 2 else (f"eu{j}", 2 + j % 2)
                        if q % 2 == 0:
                            claim(pe, key, b, job, signal=False)
                        chunk_product(c, [(0, bank[b])], xe_hi, xe_lo, 4 * (q % 2), q % 2 == 0,
                                      q % 2 == 1, W, idx=idx, slot=(N0 + c) % NSPL, done=chunk_used)
                    else:
                        i, q = divmod(c - 4 * EJ, EK // CK)
                        if q == 0:
                            claim(pe, f"ed{i}", 4 + i, job, signal=False)
                        if i == 0:
                            wait_emptied(pe, f"et{q}", job)
                        chunk_product(c, [(0, bank[4 + i])], eT_hi, eT_lo, CK * q, q == 0,
                                      q == EK // CK - 1, W, idx=idx, slot=(N0 + c) % NSPL,
                                      done=chunk_used)
                    if c % 4 == 1 and 1 <= c // 4 <= EJ:
                        j = c // 4 - 1
                        b = 6 + j % 2
                        pe.wait_ge(sem("e_hidden"), EJ * job + j + 1)
                        d = claim(pe, f"et{j}", b, job)
                        for q in range(4):
                            m = nc.tensor.transpose(d[:, q * P:(q + 1) * P],
                                                    e_h[j % 2][:, q * P:(q + 1) * P], ident[:, :])
                        m.then_inc(filled[b], 1)
                pe.wait_ge(sem("picked"), job + 2)
                gather("gB", job)
                for t in range(TB):
                    for i in range(2):
                        if t == 0:
                            wait_emptied(pe, f"ed{i}", job)
                        b = (6 + t) if i == 0 else (4 + t)
                        d = claim(pe, f"ec{i}{t}", b, job)
                        nc.tensor.matmul(d[:, :], pickT[:, t, :], y_hi[:, i * W:(i + 1) * W],
                                         start=True, stop=False)
                        nc.tensor.matmul(d[:, :], pickT[:, t, :], y_lo[:, i * W:(i + 1) * W],
                                         start=False, stop=True).then_inc(filled[b], 1)
                slots("pB", job, bass.ds(job + 1, 1))
            assert [a - b for a, b in zip(claims, before[0])] == JOB_CLAIMS
            assert [a - b for a, b in zip(signals, before[1])] == JOB_SIGNALS

        @block.sync
        def _(sp):
            sp.dma_start(X[:, :, :], x[0].rearrange("(t p) d -> p t d", p=P)).then_inc(sem("x_in"), 16)
            for c, (src, n, cols) in enumerate(chunks):
                if c == 1:
                    sp.dma_start(mem_tok[:, :, :], mem[0].rearrange("(t p) d -> p t d", p=P))\
                      .then_inc(sem("mem_in"), 16)
                if c >= NRAW:
                    sp.wait_ge(lo_made, c - NRAW + 1)
                dst = raw[c % NRAW][:, 0:n * cols].rearrange("p (k c) -> p k c", k=n)
                sp.dma_start(dst, src).then_inc(raw_in[c % NRAW], 16)

            def expert_chunks(e, job, first=False):
                for c in range(EC):
                    if first and c < NRAW:
                        sp.wait_ge(lo_made, N0 + c - NRAW + 1)
                    elif first and c == NRAW:
                        wait_filled(sp, "router0")
                    else:
                        sp.wait_ge(lo_made, N0 + c - NEXP + 1 + EC * job)
                    if c < 4 * EJ:
                        j, q = c // 4, c % 4
                        w = moe_w_gate if q < 2 else moe_w_up
                        k0, col = CK * (q % 2), j * W
                    else:
                        i, q = divmod(c - 4 * EJ, EK // CK)
                        w, k0, col = moe_w_down, CK * q, i * W
                    src = w[0][bass.ds(e, 1), k0 * P:(k0 + CK) * P, col:col + W].rearrange(
                        "e (k p) c -> p (e k) c", p=P)
                    s = c % NEXP
                    sp.dma_start(raw_exp[s][:, :].rearrange("p (k c) -> p k c", k=CK), src)\
                      .then_inc(exp_in[s], 16)

            expert_chunks(0, 0, first=True)
            with sp.Fori(1, NE) as e:
                expert_chunks(e, e)
            sp.wait_ge(sem("rounds_made"), 1)
            n_rounds = sp.value_load(rounds[0:1, 0:1], min_val=1, max_val=2)
            with sp.If(n_rounds > 1):
                with sp.Fori(0, NE) as e:
                    expert_chunks(e, e + NE)
            with sp.Else():
                sp.nop()
            for t in range(TB):
                sp.wait_ge(sem("out_made"), t + 1)
                sp.dma_start(out[0].rearrange("(t p) d -> p t d", p=P)[:, t, :], X[:, t, :])\
                  .then_inc(sem("out_done"), 16)
            sp.wait_ge(sem("out_done"), 16 * TB)

        @block.gpsimd
        def _(pool):
            def mask(dst, width, base, step, cm, fill, op=ALU.is_ge):
                return nc.gpsimd.affine_select(out=dst, in_=dst, pattern=[[step, width]],
                                               compare_op=op, fill=fill, base=base,
                                               channel_multiplier=cm)

            chain = [0]

            def link(ins):
                chain[0] += 1
                ins.then_inc(sem("pool_chain"), 1)
                pool.wait_ge(sem("pool_chain"), chain[0])

            link(nc.gpsimd.memset(ident[:, :], 0.0))
            mask(ident[:, :], P, 0, -1, 1, 1.0, ALU.not_equal).then_inc(sem("ident_made"), 1)
            pool.dma_start(sinks[:, :], ab_sinks[0].partition_broadcast(P)).then_inc(sem("sink_in"), 16)
            pool.dma_start(gate_b[:, :], c_b_f[0].partition_broadcast(P)).then_inc(sem("b_in"), 16)
            pool.dma_start(f_w[:, :, :], c_w_in[0][:, 3 * D:3 * D + CH].rearrange("(k p) c -> p k c", p=P))\
                .then_inc(sem("f_in"), 16)
            link(nc.gpsimd.memset(ones[:, :], 1.0))
            link(nc.gpsimd.memset(tri_ge[:, :], 1.0))
            link(mask(tri_ge[:, :], P, 0, -1, 1, 0.0))
            link(nc.gpsimd.memset(tri_lt[:, :], 1.0))
            mask(tri_lt[:, :], P, -1, 1, -1, 0.0).then_inc(sem("consts"), 1)
            link(nc.gpsimd.iota(dist[:, 0:P], [[-1, P]], base=0, channel_multiplier=1,
                                allow_small_or_imprecise_dtypes=True))
            link(nc.gpsimd.iota(dist[:, P:TRI], [[-1, SEQ]], base=P, channel_multiplier=1,
                                allow_small_or_imprecise_dtypes=True))
            link(nc.gpsimd.memset(b_add[:, :], 0.0))
            link(mask(b_add[:, 0:P], P, -1, 1, -1, -BIG))
            link(mask(b_add[:, SEQ:TRI], P, -1, 1, -1, -BIG))
            link(nc.gpsimd.memset(b_neg8[:, :], -1.0 / SC))
            link(mask(b_neg8[:, 0:P], P, -1, 1, -1, 0.0))
            link(mask(b_neg8[:, SEQ:TRI], P, -1, 1, -1, 0.0))
            nc.gpsimd.nop().then_inc(sem("masks0"), 1)
            pool.wait_ge(sem("dist_abs"), 1)
            link(mask(dist[:, 64:P], 64, -64, 0, 1, BIG))
            link(nc.gpsimd.memset(dist[:, P:P + 64], BIG))
            link(mask(dist[:, P + 64:SEQ], 64, 63, 0, -1, BIG))
            mask(dist[:, SEQ + 64:TRI], 64, -64, 0, 1, BIG).then_inc(sem("masks0"), 1)

            def ln_params(n):
                l, i = LNS[n]
                if i == 0:
                    pool.wait_ge(sem(f"unit_done{l}"), NU)
                else:
                    pool.wait_ge(sem("normed"), NORMED * n)
                pool.dma_start(gb[:, 0, :], ln_g[l, i].partition_broadcast(P)).then_inc(sem("ln_in"), 16)
                pool.dma_start(gb[:, 1, :], ln_b[l, i].partition_broadcast(P)).then_inc(sem("ln_in"), 16)
                pool.wait_ge(sem("ln_in"), 32 * (n + 1))

            def split(c):
                n = CHUNK if c >= N0 else chunks[c][1] * chunks[c][2]
                pool.wait_ge(lo_made, c)
                pool.wait_ge(hi_made, c + 1)
                nc.gpsimd.tensor_tensor(w_lo[c % NSPL][:, 0:n], raw[c % NRAW][:, 0:n],
                                        w_hi[c % NSPL][:, 0:n].bitcast(F32), ALU.subtract)\
                    .then_inc(lo_made, 1)

            for c in sorted(POOL_SPLIT[0]):
                split(c)
            for n in range(3):
                ln_params(n)
                split(BEHIND[n])
            wait_block(pool, "0dn1")
            link(nc.gpsimd.memset(c_add[:, :], 0.0))
            link(mask(c_add[:, 0:P], P, 0, -1, 1, -BIG))
            link(mask(c_add[:, SEQ:TRI], P, 0, -1, 1, -BIG))
            link(nc.gpsimd.memset(tri_le[:, :], 1.0))
            link(mask(tri_le[:, 0:P], P, 0, 1, -1, 0.0))
            mask(tri_le[:, P:SEQ], P, 0, 1, -1, 0.0).then_inc(sem("masks1"), 1)
            pool.wait_ge(sem("masks1"), 1)
            pool.wait_ge(sem("softp_made"), 1)
            for i in range(CH):
                if i >= 2:
                    wait_filled(pool, f"1s{i - 2}")
                for t in range(TB):
                    ins = nc.gpsimd.tensor_scalar(f_col[:, i % 2, t, :], ones[:, :],
                                                  softp[:, t, i:i + 1], None, ALU.mult)
                    if t == 0:
                        link(ins)
                ins.then_inc(sem("f_col_made"), 1)
                if i - 2 in KV_SPLIT[1]:
                    split(blocks["1kv0"][0] + KV_SPLIT[1][i - 2])
            ln_params(3)
            split(BEHIND[3])
            ln_params(4)
            for i in range(MH):
                wait_filled(pool, f"1mo{i}")
            pool.dma_start(r_w[:, :, :], moe_router[0].rearrange("(k p) e -> p k e", p=P))\
                .then_inc(sem("r_in"), 16)
            nc.gpsimd.iota(slot_no[:, :], [[1, P]], base=1, channel_multiplier=0,
                           allow_small_or_imprecise_dtypes=True).then_inc(sem("slot_made"), 1)
            split(BEHIND[4])
            for t in range(TB):
                pool.wait_ge(sem("xr_hi_made"), t + 1)
                nc.gpsimd.tensor_tensor(xr_lo[:, t, :], X[:, t, :], xr_hi[:, t, :].bitcast(F32),
                                        ALU.subtract).then_inc(sem("xr_made"), 1)
            ln_params(5)

        @block.scalar
        def _(act):
            cursor = [0]
            unused = [0]

            def copy(dst, src):
                return nc.scalar.activation(dst, src, ACT.Copy)

            def split(upto):
                while cursor[0] <= min(upto, N0 + NSPL - 1):
                    c = cursor[0]
                    cursor[0] += 1
                    if c >= N0:
                        n = CHUNK
                    else:
                        n = chunks[c][1] * chunks[c][2]
                    act.wait_ge(raw_in[c % NRAW], 16 * (c // NRAW + 1))
                    if c >= NSPL:
                        act.wait_ge(chunk_used, c - NSPL + 1)
                    copy(w_hi[c % NSPL][:, 0:n], raw[c % NRAW][:, 0:n]).then_inc(hi_made, 1)

            def preload(func):
                c = unused[0]
                unused[0] += 1
                nc.scalar.activation(warm[:, c:c + 1], ones[:, 0:1], func)

            def split_to(key, hi):
                for q in range(4):
                    b = wait_filled(act, f"{key}.{q}")
                    copy(hi[:, 2 * q:2 * q + 2, :].rearrange("p k t -> p (k t)"), b[:, :])\
                        .then_inc(sem("t_hi"), 1)

            def start_rstd(n):
                preload(ACT.Sqrt)
                for t in range(TB):
                    act.wait_ge(sem("var_made"), 2 * n + t + 1)
                    nc.scalar.activation(rstd[:, t:t + 1], rstd[:, t:t + 1], ACT.Sqrt)\
                        .then_inc(sem("rstd_made"), 1)

            def last_block(name):
                split(last_chunk(name) + 1)

            def after(name):
                split(last_chunk(name) + NSPL - 1)
                wait_block(act, name)

            def mv_evacuate(name, blk):
                wait_block(act, name)
                empties(copy(MV[:, 0, (blk - 2) * W:(blk - 1) * W], bank_of(f"{name}.0")[:, :]),
                        f"{name}.0")

            split_to("0x", xT_hi)
            split(NSPL - 1)
            split_to("m", mT_hi)
            for l in range(2):
                names = [n for n, *_ in QKV[l]]
                if l == 1:
                    act.wait_ge(sem("fu_made"), 1)
                    nc.scalar.activation(softp_t[:, :, :], softp_t[:, :, :], ACT.Exp)\
                        .then_inc(sem("act_chain"), 1)
                    act.wait_ge(sem("act_chain"), 1)
                    nc.scalar.activation(softp_t[:, :, :], softp_t[:, :, :], ACT.Ln, bias=1.0)\
                        .then_inc(sem("fl_made"), 1)

                def qk_evacuate(name, l=l):
                    b = wait_filled(act, f"{l}{name}T.0")
                    t0 = TILES[l][name]
                    empties(copy(QK[:, t0:t0 + 2, :].rearrange("p k t -> p (k t)"), b[:, :]),
                            f"{l}{name}T.0")

                for i, name in enumerate(names):
                    if i and names[i - 1] in TILES[l]:
                        split(blocks[f"{l}{name}"][0] + NSPL - 1)
                        qk_evacuate(names[i - 1])
                    after(f"{l}{name}")
                    key = f"{l}{name}.0"
                    src = bank_of(key)
                    if name in TILES[l]:
                        back = [n for n in names[:i] if n in TILES[l]]
                        if len(back) >= 2:
                            for q in range(1 if back[-2] == "akv" else 2):
                                wait_filled(act, f"{l}{back[-2]}T.{q}")
                        dst = stage[:, len(back) % 2, 0, :]
                    if name == "akv":
                        kv = dst[:, 0:2 * P].rearrange("p (h r d) -> p h r d", h=KVH, r=2)
                        s = src[:, 0:P].rearrange("p (h d) -> p h d", h=KVH)
                        copy(kv[:, :, 0, :], s)
                        copy(kv[:, :, 1, :], s)
                        empties(copy(V[:, 0, 0:P], src[:, P:2 * P]), key)
                    elif name in TILES[l]:
                        empties(copy(dst, src[:, :]), key)
                    else:
                        v0 = VALUES[l][name]
                        empties(copy(V[:, 0, v0:v0 + W], src[:, :]), key)
                us = units(l)

                def first(i, l=l, us=us):
                    kind = us[i][0]
                    S, Pb = S_t[i % 2], P_t[i % 2]
                    if kind == "B":
                        j = i - AH
                        act.wait_ge(sem(f"zc_made{l}"), j + 1)
                        nc.scalar.activation(S[:, 0:TRI], S[:, 0:TRI], ACT.Exp).then_inc(sem(f"ez{l}"), 1)
                        act.wait_ge(sem(f"ez{l}"), j + 1)
                        nc.scalar.activation(S[:, 0:TRI], S[:, 0:TRI], ACT.Ln, bias=1.0)\
                            .then_inc(sem(f"lnz_made{l}"), 1)
                        return
                    act.wait_ge(sem(f"max_made{l}"), i + 1)
                    if i >= 2:
                        wait_filled(act, f"{l}t{i - 2}")
                    for t, (a, b) in enumerate(((0, P), (P, TRI))):
                        nc.scalar.activation(Pb[:, a:b], S[:, a:b], ACT.Exp,
                                             bias=neg_max[:, i % 2, t:t + 1], scale=SC,
                                             accum_out=row_sum[:, (i // 4) % 2, t, i % 4:i % 4 + 1])\
                            .then_inc(sem(f"probs_made{l}"), 1)
                    if kind == "A":
                        nc.scalar.activation(sink_exp[:, (i // 4) % 2, :, i % 4], neg_max[:, i % 2, :],
                                             ACT.Exp, bias=sinks[:, i:i + 1])\
                            .then_inc(sem("sink_made"), 1)

                def second(i, l=l, us=us):
                    PT = PT_t[i % 2]
                    if us[i][0] == "B":
                        j = i - AH
                        act.wait_ge(sem(f"w_made{l}"), j + 1)
                        nc.scalar.activation(PT[:, 0:TRI], PT[:, 0:TRI], ACT.Exp, scale=SC)\
                            .then_inc(sem(f"aT_made{l}"), 1)
                    else:
                        b = wait_filled(act, f"{l}t{i}")
                        if i >= 2:
                            act.wait_ge(sem(f"unit_done{l}"), i - 1)
                        empties(copy(PT[:, 0:TRI], b[:, 0:TRI]), f"{l}t{i}")

                def mem_evacuate(i, l=l):
                    if i in KV_DONE[l]:
                        blk = KV_DONE[l][i]
                        name = f"{l}kv{blk}"
                        if blk >= 2:
                            mv_evacuate(name, blk)
                        else:
                            wait_block(act, name)
                            if blk == 1:
                                for q in range(2):
                                    wait_filled(act, f"{l}kv0T.{q}")
                            empties(copy(m_stage[:, 0, :], bank_of(f"{name}.0")[:, :]), f"{name}.0")
                    if i in KT_DONE[l]:
                        blk = KT_DONE[l][i]
                        name = f"{l}kv{blk}T"
                        b = wait_filled(act, f"{name}.0")
                        t0 = 4 * blk + 0
                        empties(copy(MK[:, t0:t0 + 2, :].rearrange("p k t -> p (k t)"), b[:, :]),
                                f"{name}.0")

                act.wait_ge(sem("consts"), 1)
                preload(ACT.Exp)
                for i in range(NU + 1):
                    if i < NU:
                        first(i)
                    mem_evacuate(i)
                    if i >= 1:
                        second(i - 1)
                    if i in KV_SPLIT[l]:
                        split(blocks[f"{l}kv0"][0] + KV_SPLIT[l][i])
                split_to(f"{l}oT", xT_hi)
                last_block(f"{l}out1")
                start_rstd(3 * l)
                split(last_chunk(f"{l}kv3"))
                split_to(f"{l}n0", xT_hi)
                split(last_chunk(f"{l}kv3") + NSPL - 1)
                mv_evacuate(f"{l}kv3", 3)

                def mq_evacuate(i, l=l):
                    b = wait_filled(act, f"{l}mq{i}T.0")
                    empties(copy(QK[:, 4 * i:4 * i + 2, :].rearrange("p k t -> p (k t)"), b[:, :]),
                            f"{l}mq{i}T.0")

                for i in range(2):
                    name = f"{l}mq{i}"
                    if i:
                        split(blocks[name][0] + NSPL)
                        mq_evacuate(0)
                    after(name)
                    empties(copy(stage[:, i, 0, :], bank_of(f"{name}.0")[:, :]), f"{name}.0")
                mq_evacuate(1)
                split(last_chunk(f"{l}mq1") + NSPL)
                preload(ACT.Exp)
                for h in range(MH + 1):
                    if h < MH:
                        act.wait_ge(sem(f"m_max_made{l}"), h + 1)
                        if h >= 2:
                            wait_filled(act, f"{l}mt{h - 2}")
                        b = bank_of(f"{l}ms{h}")
                        for t in range(TB):
                            ins = nc.scalar.activation(
                                P_t[h % 2][:, t * SEQ:(t + 1) * SEQ], b[:, t * SEQ:(t + 1) * SEQ],
                                ACT.Exp, bias=neg_max[:, h % 2, t:t + 1], scale=MSC,
                                accum_out=row_sum[:, 0, t, h:h + 1])
                            ins.then_inc(sem(f"m_probs_made{l}"), 1)
                        act.wait_ge(sem(f"m_probs_made{l}"), 2 * (h + 1))
                        empties(nc.scalar.nop(), f"{l}ms{h}")
                    if h >= 1:
                        i = h - 1
                        b = wait_filled(act, f"{l}mt{i}")
                        if i >= 2:
                            wait_filled(act, f"{l}mo{i - 2}")
                        empties(copy(PT_t[i % 2][:, :], b[:, :]), f"{l}mt{i}")
                split_to(f"{l}moT", xT_hi)
                if l == 1:
                    act.wait_ge(sem("r_in"), 16)
                    copy(r_hi[:, :, :], r_w[:, :, :]).then_inc(sem("r_hi"), 1)
                last_block(f"{l}mw1")
                start_rstd(3 * l + 1)
                split_to(f"{l}n1", xT_hi)
                if l == 1:
                    for t in range(TB):
                        act.wait_ge(sem("normed"), NORMED * 4 + 2 * (t + 1))
                        copy(xr_hi[:, t, :], X[:, t, :]).then_inc(sem("xr_hi_made"), 1)
                split(last_chunk(f"{l}mw1") + NSPL)

                if l == 0:
                    def h_hi(j):
                        for q in range(FB[j][1] // (2 * P)):
                            b = wait_filled(act, f"0h{j}T.{q}")
                            k = 4 * j + 2 * q
                            copy(hT_hi[:, k:k + 2, :].rearrange("p k t -> p (k t)"), b[:, :])\
                                .then_inc(sem("t_hi"), 1)

                    for j, (_, n) in enumerate(FB):
                        split(blocks[f"0g{j}"][0] + NSPL)
                        if j:
                            h_hi(j - 1)
                        after(f"0g{j}")
                        for t in range(TB):
                            if j:
                                wait_emptied(act, f"0u{j - 1}.{t}")
                            nc.scalar.activation(act_g[:, t, 0:n], bank_of(f"0g{j}.{t}")[:, 0:n],
                                                 ACT.Silu).then_inc(
                                                     emptied[fillings[f"0g{j}.{t}"][0]], 1)
                        split(last_chunk(f"0u{j}") + NSPL - 1)
                    split(blocks["0dn0"][0] + NSPL)
                    h_hi(len(FB) - 1)
                    act.wait_ge(sem("f_in"), 16)
                    copy(f_hi[:, :, :], f_w[:, :, :]).then_inc(sem("f_hi"), 1)
                    last_block("0dn1")
                    start_rstd(2)
                    split(last_chunk("1kv2"))
                    split_to("0n2", xT_hi)
                    split(last_chunk("1kv2") + NSPL - 1)
                    mv_evacuate("1kv2", 2)

            act.wait_ge(sem("gap_made"), 1)
            nc.scalar.activation(gap[:, :], gap[:, :], ACT.Exp).then_inc(sem("gap_exp"), 1)

            def gathered(tag, job):
                for half in range(2):
                    b = wait_filled(act, f"{tag}{half}", job)
                    empties(copy(xe_hi[:, 4 * half:4 * half + 4, :].rearrange("p k s -> p (k s)"),
                                 b[:, :]), f"{tag}{half}")

            gathered("gA", None)
            act.wait_ge(sem("rounds_made"), 1)
            n_rounds = act.value_load(rounds[0:1, 0:1], min_val=1, max_val=2)
            assert cursor[0] == N0 + NSPL
            with act.Fori(0, n_rounds * NE) as job:
                for c in range(EC):
                    idx = N0 + c + EC * job

                    def w_split(c=c, idx=idx):
                        n = c + NSPL
                        r, s = n % NEXP, (N0 + n) % NSPL
                        act.wait_ge(exp_in[r], 16 * (exp_before[r] + n // NEXP + 1
                                                     + EC // NEXP * job))
                        act.wait_ge(chunk_used, idx + 1)
                        copy(w_hi[s][:, :], raw_exp[r][:, :]).then_inc(hi_made, 1)

                    if c < 4 * EJ and c % 4 == 1:
                        j = c // 4
                        act.wait_ge(chunk_used, idx + 1)
                        if j >= 2:
                            act.wait_ge(sem("e_hidden"), EJ * job + j - 1)
                        nc.scalar.activation(e_g[j % 2][:, :], bank_of(f"eg{j}")[:, :], ACT.Silu)\
                            .then_inc(emptied[fillings[f"eg{j}"][0]], 1)
                    if c == 4 * EJ + EK // CK - 1 or c == EC - 1:
                        i = (c - 4 * EJ) // (EK // CK)
                        act.wait_ge(chunk_used, idx + 1)
                        nc.scalar.activation(y_hi[:, i * W:(i + 1) * W], bank_of(f"ed{i}")[:, :],
                                             ACT.Copy, scale=slot_w[:, 0:1]).then_inc(sem("y_hi_made"), 1)
                    if c < EC - NSPL:
                        w_split()
                    else:
                        with act.If(job < n_rounds * NE - 1):
                            w_split()
                        with act.Else():
                            act.nop()
                    if c % 4 == 2 and 1 <= c // 4 <= EJ:
                        j = c // 4 - 1
                        b = wait_filled(act, f"et{j}", job)
                        copy(eT_hi[:, 4 * j:4 * j + 4, :].rearrange("p k s -> p (k s)"), b[:, :])\
                            .then_inc(sem("eT_hi_made"), 1)
                gathered("gB", job)
            preload(ACT.Sqrt)
            act.wait_ge(sem("vars_made"), 1)
            nc.scalar.activation(rstd[:, :], rstd[:, :], ACT.Sqrt).then_inc(sem("rstds_made"), 1)

        @block.vector
        def _(dve):
            cursor = [0]
            chain = [0]
            t_hi = [0]
            tt = nc.vector.tensor_tensor

            def link(ins):
                chain[0] += 1
                ins.then_inc(sem("dve_chain"), 1)
                dve.wait_ge(sem("dve_chain"), chain[0])

            def copy(dst, src):
                return nc.vector.tensor_copy(dst, src)

            def split(upto):
                while cursor[0] <= min(upto, N0 + NSPL - 1):
                    c = cursor[0]
                    cursor[0] += 1
                    if c in BY_POOL:
                        continue
                    if c - 1 in BY_POOL:
                        dve.wait_ge(lo_made, c)
                    n = CHUNK if c >= N0 else chunks[c][1] * chunks[c][2]
                    dve.wait_ge(hi_made, c + 1)
                    tt(w_lo[c % NSPL][:, 0:n], raw[c % NRAW][:, 0:n],
                       w_hi[c % NSPL][:, 0:n].bitcast(F32), ALU.subtract).then_inc(lo_made, 1)

            def rest(dst, b, hi, key):
                t_hi[0] += 1
                dve.wait_ge(sem("t_hi"), t_hi[0])
                empties(tt(dst, b[:, :], hi.bitcast(F32), ALU.subtract), key)

            def split_to(key, hi, lo):
                for q in range(4):
                    flat = "p k t -> p (k t)"
                    rest(lo[:, 2 * q:2 * q + 2, :].rearrange(flat), bank_of(f"{key}.{q}"),
                         hi[:, 2 * q:2 * q + 2, :].rearrange(flat), f"{key}.{q}")

            def after(name):
                split(last_chunk(name) + NSPL - 1)
                wait_block(dve, name)

            def add_residual(name, half, t):
                key = f"{name}.{t}"
                xs = X[:, t, half * W:(half + 1) * W]
                empties(nc.vector.scalar_tensor_tensor(out=xs, in0=xs, scalar=ALPHA,
                                                       in1=bank_of(key)[:, :], op0=ALU.mult,
                                                       op1=ALU.add), key)
                wait_emptied(dve, key)
                link(nc.vector.bn_stats(stats[:, t, half, :], xs))

            def norm(n, t):
                xt, r, w = X[:, t, :], rstd[:, t:t + 1], newton[:, t:t + 1]
                v = var_eps[:, t:t + 1]
                link(nc.vector.bn_aggr(mean_var[:, t, :],
                                       stats[:, t, :, :].rearrange("p a b -> p (a b)")))
                link(nc.vector.tensor_scalar(v, mean_var[:, t, 1:2], LN_EPS, None, ALU.add))
                nc.vector.reciprocal(r, v).then_inc(sem("var_made"), 1)
                dve.wait_ge(sem("ln_in"), 32 * (n + 1))
                link(nc.vector.scalar_tensor_tensor(out=xt, in0=xt, scalar=mean_var[:, t, 0:1],
                                                    in1=gb[:, 0, :], op0=ALU.subtract, op1=ALU.mult))
                dve.wait_ge(sem("rstd_made"), 2 * n + t + 1)
                link(nc.vector.tensor_scalar(w, r, r, v, ALU.mult, ALU.mult))
                link(nc.vector.tensor_scalar(w, w, -0.5, 1.5, ALU.mult, ALU.add))
                link(tt(r, r, w, ALU.mult))
                for half in range(2):
                    c = slice(half * W, (half + 1) * W)
                    nc.vector.scalar_tensor_tensor(out=xt[:, c], in0=xt[:, c], scalar=r,
                                                   in1=gb[:, 1, c], op0=ALU.mult, op1=ALU.add)\
                        .then_inc(sem("normed"), 1)

            def end_sublayer(names, n):
                after(names[0])
                for t in range(TB):
                    add_residual(names[0], 0, t)
                split(last_chunk(names[1]) + 1)
                for t in range(TB):
                    if t == 0:
                        wait_filled(dve, f"{names[1]}.0")
                    else:
                        wait_block(dve, names[1])
                    add_residual(names[1], 1, t)
                    norm(n, t)

            def stage_narrow(key, n, sb, staged):
                b = wait_filled(dve, key)
                link(copy(sb[0:n, 0:SEQ], b[0:n, 0:SEQ]))
                nc.vector.nop().then_inc(emptied[4], 1)
                nc.vector.nop().then_inc(sem(staged), 1)

            def mv_evacuate(name, blk):
                wait_block(dve, name)
                empties(copy(MV[:, 1, (blk - 2) * W:(blk - 1) * W], bank_of(f"{name}.1")[:, :]),
                        f"{name}.1")

            split_to("0x", xT_hi, xT_lo)
            split(NSPL - 1)
            split_to("m", mT_hi, mT_lo)
            dve.wait_ge(sem("masks0"), 1)
            nc.vector.scalar_tensor_tensor(out=dist[:, :], in0=dist[:, :], scalar=-1.0, in1=dist[:, :],
                                           op0=ALU.mult, op1=ALU.max)\
                .then_inc(sem("dist_abs"), 1)
            dve.wait_ge(sem("sink_in"), 16)
            link(nc.vector.tensor_scalar(neg_sinks[:, :], sinks[:, :], -1.0, None, ALU.mult))

            for l in range(2):
                names = [n for n, *_ in QKV[l]]
                if l == 1:
                    stage_narrow("f0", CH, P_t[0], "f_T_made")
                    b = wait_filled(dve, "f")
                    dve.wait_ge(sem("b_in"), 16)
                    for t in range(TB):
                        ins = tt(softp[:, t, :], b[:, t * CH:(t + 1) * CH], gate_b[:, :], ALU.add)
                        if t == 0:
                            link(ins)
                    empties(ins, "f")
                    wait_emptied(dve, "f")
                    link(nc.vector.tensor_scalar(softp[:, :, :], softp[:, :, :], -1.0, None, ALU.mult))
                    nc.vector.tensor_scalar(softp_t[:, :, :], softp[:, :, :], 40.0, None, ALU.min)\
                        .then_inc(sem("fu_made"), 1)
                    dve.wait_ge(sem("fl_made"), 1)
                    link(tt(softp[:, :, :], softp[:, :, :], softp_t[:, :, :], ALU.max))
                    nc.vector.tensor_scalar(softp[:, :, :], softp[:, :, :], 1.0 / SC, None, ALU.mult)\
                        .then_inc(sem("softp_made"), 1)

                def qk_evacuate(name, l=l):
                    if name == "akv":
                        return
                    b = wait_filled(dve, f"{l}{name}T.1")
                    t0 = TILES[l][name] + 2
                    empties(copy(QK[:, t0:t0 + 2, :].rearrange("p k t -> p (k t)"), b[:, :]),
                            f"{l}{name}T.1")

                for i, name in enumerate(names):
                    if i and names[i - 1] in TILES[l]:
                        split(blocks[f"{l}{name}"][0] + NSPL - 1)
                        qk_evacuate(names[i - 1])
                    after(f"{l}{name}")
                    key = f"{l}{name}.1"
                    src = bank_of(key)
                    if name in TILES[l]:
                        back = [n for n in names[:i] if n in TILES[l]]
                        if len(back) >= 2:
                            for q in range(1 if back[-2] == "akv" else 2):
                                wait_filled(dve, f"{l}{back[-2]}T.{q}")
                        dst = stage[:, len(back) % 2, 1, :]
                    if name == "akv":
                        kv = dst[:, 0:2 * P].rearrange("p (h r d) -> p h r d", h=KVH, r=2)
                        s = src[:, 0:P].rearrange("p (h d) -> p h d", h=KVH)
                        copy(kv[:, :, 0, :], s)
                        copy(kv[:, :, 1, :], s)
                        empties(copy(V[:, 1, 0:P], src[:, P:2 * P]), key)
                    elif name in TILES[l]:
                        empties(copy(dst, src[:, :]), key)
                    else:
                        v0 = VALUES[l][name]
                        empties(copy(V[:, 1, v0:v0 + W], src[:, :]), key)
                dve.wait_ge(sem(f"masks{l}"), 2 - l)
                us = units(l)

                def first(i, l=l, us=us):
                    kind, h = us[i][0], us[i][5]
                    S, key = S_t[i % 2], f"{l}s{i}"
                    b = wait_filled(dve, key)
                    if kind == "B":
                        if i < AH + 2:
                            dve.wait_ge(sem(f"probs_made{l}"), 2 * (i - 1))
                        nc.vector.tensor_scalar(S[:, 0:TRI], b[:, 0:TRI], SC, 40.0, ALU.mult, ALU.min)\
                            .then_inc(sem(f"zc_made{l}"), 1)
                        return
                    if i >= 2:
                        dve.wait_ge(sem(f"probs_made{l}"), 2 * (i - 1))
                    if kind == "A":
                        slope = 2.0 ** (-8.0 * (h + 1) / AH)
                        empties(nc.vector.scalar_tensor_tensor(
                            out=S[:, 0:TRI], in0=dist[:, :], scalar=-slope / SC, in1=b[:, 0:TRI],
                            op0=ALU.mult, op1=ALU.add), key)
                    else:
                        empties(tt(S[:, 0:TRI], b[:, 0:TRI], c_add[:, :], ALU.add), key)
                    wait_emptied(dve, key)
                    if kind == "A" and i >= 2:
                        dve.wait_ge(sem("sink_made"), i - 1)
                    nc.vector.tensor_reduce(row_max[:, i % 2, 0:1], S[:, 0:P], AX_X, ALU.max)
                    link(nc.vector.tensor_reduce(row_max[:, i % 2, 1:2], S[:, P:TRI], AX_X, ALU.max))
                    if kind == "A":
                        nc.vector.tensor_scalar(neg_max[:, i % 2, :], row_max[:, i % 2, :], -SC,
                                                neg_sinks[:, h:h + 1], ALU.mult, ALU.min)\
                            .then_inc(sem(f"max_made{l}"), 1)
                    else:
                        nc.vector.tensor_scalar(neg_max[:, i % 2, :], row_max[:, i % 2, :], -SC, None,
                                                ALU.mult).then_inc(sem(f"max_made{l}"), 1)

                def first_end(i, l=l, us=us):
                    if us[i][0] != "B":
                        return
                    j, S, key = i - AH, S_t[i % 2], f"{l}s{i}"
                    dve.wait_ge(sem(f"lnz_made{l}"), j + 1)
                    link(nc.vector.scalar_tensor_tensor(out=S[:, 0:TRI], in0=bank_of(key)[:, 0:TRI],
                                                        scalar=SC, in1=S[:, 0:TRI], op0=ALU.mult,
                                                        op1=ALU.max))
                    nc.vector.nop().then_inc(emptied[fillings[key][0]], 1)
                    wait_filled(dve, f"{l}t{i - 2}")
                    tt(P_t[i % 2][:, 0:TRI], S[:, 0:TRI], b_neg8[:, :], ALU.mult)\
                        .then_inc(sem(f"logs_made{l}"), 1)

                def second(i, l=l, us=us):
                    if us[i][0] != "B":
                        return
                    key = f"{l}t{i}"
                    b = wait_filled(dve, key)
                    dve.wait_ge(sem(f"unit_done{l}"), i - 1)
                    link(tt(PT_t[i % 2][:, 0:TRI], b[:, 0:TRI], b_add[:, :], ALU.add))
                    nc.vector.nop().then_inc(emptied[fillings[key][0]], 1)
                    nc.vector.nop().then_inc(sem(f"w_made{l}"), 1)

                def outputs(g, l=l, us=us):
                    dve.wait_ge(sem(f"unit_done{l}"), 4 * g + 4)
                    kind = us[4 * g][0]
                    src = bank[7][:, :].rearrange("p (t u d) -> p t u d", t=TB, u=4)
                    dst = O[:, :, g * 4 * DH:(g + 1) * 4 * DH].rearrange("p t (u d) -> p t u d", u=4)
                    if kind == "B":
                        ins = copy(dst, src)
                    else:
                        rs = row_sum[:, g % 2, :, :]
                        if kind == "A":
                            dve.wait_ge(sem("sink_made"), 4 * g + 4)
                            link(tt(row_inv[:, :, :], rs, sink_exp[:, g % 2, :, :], ALU.add))
                            link(nc.vector.reciprocal(row_inv[:, :, :], row_inv[:, :, :]))
                        else:
                            link(nc.vector.reciprocal(row_inv[:, :, :], rs))
                        inv = row_inv[:, :, :].unsqueeze(3).broadcast_to([P, TB, 4, DH])
                        ins = tt(dst, src, inv, ALU.mult)
                    link(ins)
                    nc.vector.nop().then_inc(emptied[7], 1)
                    nc.vector.nop().then_inc(sem(f"o_made{l}"), 1)

                def mem_evacuate(i, l=l):
                    if i in KV_DONE[l]:
                        blk = KV_DONE[l][i]
                        name = f"{l}kv{blk}"
                        if blk >= 2:
                            mv_evacuate(name, blk)
                        else:
                            wait_block(dve, name)
                            if blk == 1:
                                for q in range(2):
                                    wait_filled(dve, f"{l}kv0T.{q}")
                            empties(copy(m_stage[:, 1, :], bank_of(f"{name}.1")[:, :]), f"{name}.1")
                    if i in KT_DONE[l]:
                        blk = KT_DONE[l][i]
                        name = f"{l}kv{blk}T"
                        b = wait_filled(dve, f"{name}.1")
                        t0 = 4 * blk + 2
                        empties(copy(MK[:, t0:t0 + 2, :].rearrange("p k t -> p (k t)"), b[:, :]),
                                f"{name}.1")

                for i in range(NU + 2):
                    if i < NU:
                        first(i)
                    mem_evacuate(i)
                    if 1 <= i <= NU:
                        second(i - 1)
                    if i < NU:
                        first_end(i)
                    if i >= 2 and (i - 2) % 4 == 3:
                        outputs((i - 2) // 4)
                split_to(f"{l}oT", xT_hi, xT_lo)
                end_sublayer([f"{l}out0", f"{l}out1"], 3 * l)
                split(last_chunk(f"{l}kv3"))
                split_to(f"{l}n0", xT_hi, xT_lo)
                split(last_chunk(f"{l}kv3") + NSPL - 1)
                mv_evacuate(f"{l}kv3", 3)

                def mq_evacuate(i, l=l):
                    b = wait_filled(dve, f"{l}mq{i}T.1")
                    empties(copy(QK[:, 4 * i + 2:4 * i + 4, :].rearrange("p k t -> p (k t)"), b[:, :]),
                            f"{l}mq{i}T.1")

                for i in range(2):
                    name = f"{l}mq{i}"
                    if i:
                        split(blocks[name][0] + NSPL)
                        mq_evacuate(0)
                    after(name)
                    empties(copy(stage[:, i, 1, :], bank_of(f"{name}.1")[:, :]), f"{name}.1")
                mq_evacuate(1)
                split(last_chunk(f"{l}mq1") + NSPL)
                for h in range(MH + 2):
                    if h < MH:
                        b = wait_filled(dve, f"{l}ms{h}")
                        if h >= 2:
                            dve.wait_ge(sem(f"m_probs_made{l}"), 2 * (h - 1))
                        link(nc.vector.tensor_reduce(row_max[:, h % 2, :],
                                                     b[:, :].rearrange("p (t s) -> p t s", t=TB),
                                                     AX_X, ALU.max))
                        nc.vector.tensor_scalar(neg_max[:, h % 2, :], row_max[:, h % 2, :], -MSC, None,
                                                ALU.mult).then_inc(sem(f"m_max_made{l}"), 1)
                    if h >= 2:
                        i = h - 2
                        b = wait_filled(dve, f"{l}mo{i}")
                        link(nc.vector.reciprocal(row_inv[:, :, i], row_sum[:, 0, :, i]))
                        for t in range(TB):
                            ins = nc.vector.tensor_scalar(O[:, t, i * MDH:(i + 1) * MDH],
                                                          b[:, t * MDH:(t + 1) * MDH],
                                                          row_inv[:, t, i:i + 1], None, ALU.mult)
                            if t == 0:
                                link(ins)
                        empties(ins, f"{l}mo{i}")
                split_to(f"{l}moT", xT_hi, xT_lo)
                if l == 1:
                    dve.wait_ge(sem("r_hi"), 1)
                    tt(r_lo[:, :, :], r_w[:, :, :], r_hi[:, :, :].bitcast(F32), ALU.subtract)\
                        .then_inc(sem("r_split"), 1)
                end_sublayer([f"{l}mw0", f"{l}mw1"], 3 * l + 1)
                split_to(f"{l}n1", xT_hi, xT_lo)
                if l == 0:
                    split(last_chunk(f"{l}mw1") + NSPL)

                if l == 0:
                    def h_lo(j):
                        for q in range(FB[j][1] // (2 * P)):
                            k = 4 * j + 2 * q
                            flat = "p k t -> p (k t)"
                            rest(hT_lo[:, k:k + 2, :].rearrange(flat), bank_of(f"0h{j}T.{q}"),
                                 hT_hi[:, k:k + 2, :].rearrange(flat), f"0h{j}T.{q}")

                    for j, (_, n) in enumerate(FB):
                        split(blocks[f"0g{j}"][0] + NSPL)
                        if j:
                            h_lo(j - 1)
                        split(last_chunk(f"0u{j}") + NSPL - 1)
                        wait_block(dve, f"0u{j}")
                        for t in range(TB):
                            wait_emptied(dve, f"0g{j}.{t}")
                            if j >= 2:
                                for q in range(2):
                                    wait_filled(dve, f"0h{j - 2}T.{q}")
                            empties(tt(h_tok[j % 2][:, t, 0:n], bank_of(f"0u{j}.{t}")[:, 0:n],
                                       act_g[:, t, 0:n], ALU.mult), f"0u{j}.{t}")
                    split(blocks["0dn0"][0] + NSPL)
                    h_lo(len(FB) - 1)
                    dve.wait_ge(sem("f_hi"), 1)
                    tt(f_lo[:, :, :], f_w[:, :, :], f_hi[:, :, :].bitcast(F32), ALU.subtract)\
                        .then_inc(sem("f_split"), 1)
                    end_sublayer(["0dn0", "0dn1"], 2)
                    split(last_chunk("1kv2"))
                    split_to("0n2", xT_hi, xT_lo)
                    split(last_chunk("1kv2") + NSPL - 1)
                    mv_evacuate("1kv2", 2)

            dve.wait_ge(sem("slot_made"), 1)
            stage_narrow("router0", NE, e_h[0], "r_T_made")
            b = wait_filled(dve, "router")
            link(copy(logit[:, :, :].rearrange("p t e -> p (t e)"), b[:, 0:TB * NE]))
            nc.vector.nop().then_inc(emptied[5], 1)
            nc.vector.max(best[:, 0, :], logit[:, 0, :])
            link(nc.vector.max(best[:, 1, :], logit[:, 1, :]))
            nc.vector.max_index(best_i[:, 0, :], best[:, 0, :], logit[:, 0, :])
            link(nc.vector.max_index(best_i[:, 1, :], best[:, 1, :], logit[:, 1, :]))
            link(nc.vector.tensor_scalar(best_f[:, :, :], best_i[:, :, :], 1.0, None, ALU.add))
            expert = slot_no[:, 0:NE].unsqueeze(1).broadcast_to([P, TB, NE])
            tt(hot1[:, :, :], expert, best_f[:, :, 0:1].broadcast_to([P, TB, NE]), ALU.is_equal)
            link(tt(hot2[:, :, :], expert, best_f[:, :, 1:2].broadcast_to([P, TB, NE]), ALU.is_equal))
            tt(taken[:, :, :], hot1[:, :, :], hot2[:, :, :], ALU.add).then_inc(sem("taken_made"), 1)
            tt(gap[:, :], best[:, :, 1], best[:, :, 0], ALU.subtract).then_inc(sem("gap_made"), 1)
            nc.vector.memset(wt[:, :, :], 0.0)
            link(nc.vector.memset(place[:, :, :], 0.0))
            b = wait_filled(dve, "places")
            link(nc.vector.scalar_tensor_tensor(
                out=place[:, :, 0:NE], in0=b[:, 0:2 * NE].rearrange("p (t e) -> p t e", t=TB), scalar=1.0,
                in1=taken[:, :, :], op0=ALU.add, op1=ALU.mult))

            def picks(nxt):
                for t in range(TB):
                    ins = nc.vector.tensor_scalar(pick[:, t, :], slot_no[:, :], place[:, t, nxt], None,
                                                  ALU.is_equal)
                ins.then_inc(sem("picked"), 1)

            picks(slice(0, 1))
            dve.wait_ge(sem("gap_exp"), 1)
            link(nc.vector.tensor_scalar(g1[:, :], gap[:, :], 1.0, None, ALU.add))
            link(nc.vector.reciprocal(g1[:, :], g1[:, :]))
            link(tt(g2[:, :], g1[:, :], gap[:, :], ALU.mult))
            for t in range(TB):
                link(nc.vector.tensor_scalar(hot2[:, t, :], hot2[:, t, :], g2[:, t:t + 1], None,
                                             ALU.mult))
                link(nc.vector.scalar_tensor_tensor(out=wt[:, t, 0:NE], in0=hot1[:, t, :],
                                                    scalar=g1[:, t:t + 1], in1=hot2[:, t, :],
                                                    op0=ALU.mult, op1=ALU.add))
            copy(wt[:, :, NE:2 * NE], wt[:, :, 0:NE]).then_inc(sem("gates_made"), 1)
            nc.vector.tensor_scalar(place[:, :, NE:2 * NE], place[:, :, 0:NE], -float(P), None, ALU.add)
            link(nc.vector.tensor_reduce(most[:, :], bank_of("places")[:, 2 * NE:3 * NE], AX_X, ALU.max))
            nc.vector.nop().then_inc(emptied[4], 1)
            link(nc.vector.tensor_scalar(most[:, :], most[:, :], float(P), 1.0, ALU.is_gt, ALU.add))
            copy(rounds[:, :], most[:, :]).then_inc(sem("rounds_made"), 1)

            def gathered(tag, job):
                for half in range(2):
                    b = wait_filled(dve, f"{tag}{2 + half}", job)
                    empties(copy(xe_lo[:, 4 * half:4 * half + 4, :].rearrange("p k s -> p (k s)"),
                                 b[:, :]), f"{tag}{2 + half}")

            def slots(tag, job, n):
                b = wait_filled(dve, tag, job)
                copy(pickT[:, :, :].rearrange("p t s -> p (t s)"), b[:, 0:2 * P])
                empties(copy(slot_w[:, :], b[:, 2 * P:2 * P + 1]), tag)

            split(N0 + 1)
            gathered("gA", None)
            slots("pA", None, 0)
            split(N0 + NSPL - 1)
            link(nc.vector.tensor_scalar(X[:, :, :], X[:, :, :], ALPHA, None, ALU.mult))
            n_rounds = dve.value_load(rounds[0:1, 0:1], min_val=1, max_val=2)
            with dve.Fori(0, n_rounds * NE) as job:
                for c in range(EC):
                    idx = N0 + c + EC * job
                    if c < 4 * EJ and c % 4 == 3:
                        j = c // 4
                        dve.wait_ge(chunk_used, idx + 1)
                        wait_emptied(dve, f"eg{j}", job)
                        if j >= 2:
                            wait_filled(dve, f"et{j - 2}", job)
                        ins = tt(e_h[j % 2][:, :], bank_of(f"eu{j}")[:, :], e_g[j % 2][:, :], ALU.mult)
                        ins.then_inc(sem("e_hidden"), 1)
                        dve.wait_ge(sem("e_hidden"), EJ * job + j + 1)
                        nc.vector.nop().then_inc(emptied[fillings[f"eu{j}"][0]], 1)
                    if c == 4 * EJ + EK // CK - 1 or c == EC - 1:
                        i = (c - 4 * EJ) // (EK // CK)
                        dve.wait_ge(sem("y_hi_made"), 2 * job + i + 1)
                        empties(nc.vector.scalar_tensor_tensor(
                            out=y_lo[:, i * W:(i + 1) * W], in0=bank_of(f"ed{i}")[:, :],
                            scalar=slot_w[:, 0:1], in1=y_hi[:, i * W:(i + 1) * W].bitcast(F32),
                            op0=ALU.mult, op1=ALU.subtract), f"ed{i}")

                    def w_split(c=c, idx=idx):
                        n = c + NSPL
                        r, s = n % NEXP, (N0 + n) % NSPL
                        dve.wait_ge(hi_made, idx + NSPL + 1)
                        tt(w_lo[s][:, :], raw_exp[r][:, :], w_hi[s][:, :].bitcast(F32),
                           ALU.subtract).then_inc(lo_made, 1)

                    if c < EC - NSPL:
                        w_split()
                    else:
                        with dve.If(job < n_rounds * NE - 1):
                            w_split()
                        with dve.Else():
                            dve.nop()
                    if c % 4 == 2 and 1 <= c // 4 <= EJ:
                        j = c // 4 - 1
                        dve.wait_ge(sem("eT_hi_made"), EJ * job + j + 1)
                        empties(tt(eT_lo[:, 4 * j:4 * j + 4, :].rearrange("p k s -> p (k s)"),
                                   bank_of(f"et{j}")[:, :],
                                   eT_hi[:, 4 * j:4 * j + 4, :].rearrange("p k s -> p (k s)").bitcast(F32),
                                   ALU.subtract), f"et{j}")
                    if c == 4 * EJ:
                        picks(bass.ds(job + 1, 1))
                gathered("gB", job)
                for t in range(TB):
                    for i in range(2):
                        key = f"ec{i}{t}"
                        b = wait_filled(dve, key, job)
                        xs = X[:, t, i * W:(i + 1) * W]
                        empties(tt(xs, xs, b[:, :], ALU.add), key)
                slots("pB", job, 1)
            for t in range(TB):
                for half in range(2):
                    wait_emptied(dve, f"ec{half}{t}", n_rounds * NE - 1)
                    ins = nc.vector.bn_stats(stats[:, t, half, :], X[:, t, half * W:(half + 1) * W])
            link(ins)
            for t in range(TB):
                ins = nc.vector.bn_aggr(mean_var[:, t, :],
                                        stats[:, t, :, :].rearrange("p a b -> p (a b)"))
            link(ins)
            link(nc.vector.tensor_scalar(var_eps[:, :], mean_var[:, :, 1], LN_EPS, None, ALU.add))
            nc.vector.reciprocal(rstd[:, :], var_eps[:, :]).then_inc(sem("vars_made"), 1)
            dve.wait_ge(sem("ln_in"), 32 * 6)

            def centre(t):
                return nc.vector.scalar_tensor_tensor(
                    out=X[:, t, :], in0=X[:, t, :], scalar=mean_var[:, t, 0:1], in1=gb[:, 0, :],
                    op0=ALU.subtract, op1=ALU.mult)

            centre(0)
            dve.wait_ge(sem("rstds_made"), 1)
            link(tt(newton[:, :], rstd[:, :], rstd[:, :], ALU.mult))
            link(tt(newton[:, :], newton[:, :], var_eps[:, :], ALU.mult))
            link(nc.vector.tensor_scalar(newton[:, :], newton[:, :], -0.5, 1.5, ALU.mult, ALU.add))
            link(tt(rstd[:, :], rstd[:, :], newton[:, :], ALU.mult))
            for t in range(TB):
                if t:
                    link(centre(t))
                nc.vector.scalar_tensor_tensor(out=X[:, t, :], in0=X[:, t, :], scalar=rstd[:, t:t + 1],
                                               in1=gb[:, 1, :], op0=ALU.mult, op1=ALU.add)\
                    .then_inc(sem("out_made"), 1)


_INS = ["x", "mem", "ln_g", "ln_b", "mem_wq", "mem_wkv", "mem_wo", "ab_w_in", "ab_sinks", "ab_w_out",
        "c_w_in", "c_b_f", "c_w_out", "ffn_w_gate", "ffn_w_up", "ffn_w_down",
        "moe_router", "moe_w_gate", "moe_w_up", "moe_w_down"]


def kernel(**inputs):
    import numpy as _np
    import concourse.bacc as _bacc
    from concourse import mybir as _mybir
    from concourse.bass_utils import run_bass_kernel_spmd as _run

    nc = _bacc.Bacc("TRN2", target_bir_lowering=False, num_devices=1)
    arrays, args = {}, []
    for name in _INS:
        a = _np.ascontiguousarray(inputs[name])
        arrays[f"in_{name}_dram"] = a
        args.append(nc.dram_tensor(f"in_{name}_dram", a.shape, _mybir.dt.from_np(a.dtype),
                                   kind="ExternalInput").ap())
    shape = inputs["x"].shape
    args.append(nc.dram_tensor("out_0_dram", shape, _mybir.dt.float32, kind="ExternalOutput").ap())
    trunk(nc, *args)
    r = _run(nc, [arrays], core_ids=[0])
    return r.results[0]["out_0_dram"]
```
